# Optimizing a Trainium2 kernel written in Bass

```python
import jax, jax.numpy as jnp
from jax import lax
import numpy as np

D_MODEL = 1024
BATCH = 1
SEQ = 2048
DEPTH = 2

CONV_WIDTH = 512
CONV_K = 3
POOL_WINDOWS = (2, 4, 8, 16)
POOL_WIDTH = 512
POOL_GROUP = POOL_WIDTH // len(POOL_WINDOWS)
EVEN_SIZES = (CONV_WIDTH, CONV_WIDTH, CONV_WIDTH, CONV_WIDTH, POOL_WIDTH, POOL_WIDTH)
EVEN_IN = sum(EVEN_SIZES)
EVEN_OUT = CONV_WIDTH + POOL_WIDTH

ATT_HEADS = 8
ATT_KV_HEADS = 2
ATT_HEAD_DIM = 64
ATT_WIDTH = ATT_HEADS * ATT_HEAD_DIM
ATT_KV_WIDTH = ATT_KV_HEADS * ATT_HEAD_DIM
WINDOW = 128
BLOCK = 128
MLSTM_HEADS = 4
MLSTM_QK_DIM = 64
MLSTM_V_DIM = 128
MLSTM_QK_WIDTH = MLSTM_HEADS * MLSTM_QK_DIM
MLSTM_WIDTH = MLSTM_HEADS * MLSTM_V_DIM
CHUNK = 64
ODD_SIZES = (ATT_WIDTH, ATT_KV_WIDTH, ATT_KV_WIDTH, ATT_WIDTH,
             MLSTM_QK_WIDTH, MLSTM_QK_WIDTH, MLSTM_WIDTH, MLSTM_HEADS, MLSTM_HEADS,
             MLSTM_WIDTH, MLSTM_WIDTH)
ODD_IN = sum(ODD_SIZES)
ODD_OUT = ATT_WIDTH + MLSTM_WIDTH

N_EVEN = (DEPTH + 1) // 2
N_ODD = DEPTH // 2
RMS_EPS = 1e-6

kernel_name = "hybrid_conv_pool_swa_mlstm_trunk"

def rmsnorm(x, g):
    xf = x.astype(jnp.float32)
    y = xf * lax.rsqrt(jnp.mean(xf * xf, axis=-1, keepdims=True) + RMS_EPS)
    return (y * g.astype(jnp.float32)).astype(x.dtype)

def split_cols(p, sizes):
    idx = np.cumsum(sizes)[:-1].tolist()
    return jnp.split(p, idx, axis=-1)

def alibi_slopes(n):
    return jnp.asarray([2.0 ** (-8.0 * (h + 1) / n) for h in range(n)], dtype=jnp.float32)

def short_conv_mixer(xa, bg, cg, conv_w):
    u = cg * xa
    y = lax.conv_general_dilated(
        u, conv_w[:, None, :].astype(u.dtype), window_strides=(1,),
        padding=[(CONV_K - 1, 0)], dimension_numbers=('NWC', 'WIO', 'NWC'),
        feature_group_count=u.shape[-1])
    return bg * y

def pool_mixer(u, pool_w, pool_scale):
    S = u.shape[1]
    t1 = jnp.arange(1, S + 1, dtype=jnp.float32)[None, :, None]
    outs = []
    for ug, w in zip(jnp.split(u, len(POOL_WINDOWS), axis=-1), POOL_WINDOWS):
        uf = ug.astype(jnp.float32)
        cs = jnp.cumsum(uf, axis=1)
        cs_lag = jnp.pad(cs, ((0, 0), (w, 0), (0, 0)))[:, :S]
        outs.append(((cs - cs_lag) / jnp.minimum(t1, float(w)) - uf).astype(u.dtype))
    d = jnp.stack(outs, axis=2)
    y = jnp.einsum('bsgc,gcd->bsgd', d, pool_w).reshape(u.shape)
    return y * pool_scale

def sliding_window_attention(q, k, v, sinks):
    B, S = q.shape[0], q.shape[1]
    NB = S // BLOCK
    R = ATT_HEADS // ATT_KV_HEADS
    qb = q.reshape(B, NB, BLOCK, ATT_KV_HEADS, R, ATT_HEAD_DIM)

    def with_prev(t):
        tb = t.reshape(B, NB, BLOCK, ATT_KV_HEADS, ATT_HEAD_DIM)
        prev = jnp.pad(tb, ((0, 0), (1, 0), (0, 0), (0, 0), (0, 0)))[:, :NB]
        return jnp.concatenate([prev, tb], axis=2)

    kk, vv = with_prev(k), with_prev(v)
    s = jnp.einsum('bnqgrd,bnkgd->bngrqk', qb, kk).astype(jnp.float32) * (ATT_HEAD_DIM ** -0.5)
    qi = jnp.arange(BLOCK)[:, None]
    kj = jnp.arange(2 * BLOCK)[None, :]
    dist = qi + BLOCK - kj
    in_window = (dist >= 0) & (dist < WINDOW)
    key_valid = (jnp.arange(NB)[:, None, None] > 0) | (kj >= BLOCK)[None]
    mask = in_window[None] & key_valid
    slopes = alibi_slopes(ATT_HEADS).reshape(ATT_KV_HEADS, R)
    s = s - slopes[:, :, None, None] * dist.astype(jnp.float32)
    s = jnp.where(mask[None, :, None, None], s, -jnp.inf)
    sink = jnp.broadcast_to(sinks.astype(jnp.float32).reshape(ATT_KV_HEADS, R)[:, :, None, None],
                            s.shape[:-1] + (1,))
    p = jax.nn.softmax(jnp.concatenate([s, sink], axis=-1), axis=-1)[..., :-1]
    o = jnp.einsum('bngrqk,bnkgd->bnqgrd', p.astype(vv.dtype), vv)
    return o.reshape(B, S, ATT_WIDTH)

def mlstm(q, k, v, i_pre, f_pre):
    B, S = q.shape[0], q.shape[1]
    H, L = MLSTM_HEADS, CHUNK
    NC = S // L
    f32 = jnp.float32

    def chunk(t):
        t = t.astype(f32).reshape((B, NC, L) + t.shape[2:])
        return jnp.moveaxis(t, 3, 1)

    qc = chunk(q) * (MLSTM_QK_DIM ** -0.5)
    kc, vc, ic = chunk(k), chunk(v), chunk(i_pre)
    b = jnp.cumsum(jax.nn.log_sigmoid(chunk(f_pre)), axis=-1)
    bL = b[..., -1]
    a = bL[..., None] - b + ic
    m_chunk = jnp.max(a, axis=-1)
    w = jnp.exp(a - m_chunk[..., None])
    Kc = jnp.einsum('bhcl,bhcld,bhcle->bhcde', w, kc, vc)
    Nc = jnp.einsum('bhcl,bhcld->bhcd', w, kc)

    def step(carry, inp):
        C, n, m = carry
        bL_c, m_c, K_c, N_c = inp
        m_new = jnp.maximum(bL_c + m, m_c)
        decay = jnp.exp(bL_c + m - m_new)
        sc = jnp.exp(m_c - m_new)
        C_new = decay[..., None, None] * C + sc[..., None, None] * K_c
        n_new = decay[..., None] * n + sc[..., None] * N_c
        return (C_new, n_new, m_new), (C, n, m)

    init = (jnp.zeros((B, H, MLSTM_QK_DIM, MLSTM_V_DIM), f32),
            jnp.zeros((B, H, MLSTM_QK_DIM), f32),
            jnp.zeros((B, H), f32))
    xs = (jnp.moveaxis(bL, 2, 0), jnp.moveaxis(m_chunk, 2, 0),
          jnp.moveaxis(Kc, 2, 0), jnp.moveaxis(Nc, 2, 0))
    _, (Cp, Np, Mp) = lax.scan(step, init, xs)
    Cp, Np, Mp = jnp.moveaxis(Cp, 0, 2), jnp.moveaxis(Np, 0, 2), jnp.moveaxis(Mp, 0, 2)

    g = b + Mp[..., None]
    Dm = b[..., :, None] - b[..., None, :] + ic[..., None, :]
    Dm = jnp.where(jnp.tril(jnp.ones((L, L), bool)), Dm, -jnp.inf)
    m_t = jnp.maximum(g, jnp.max(Dm, axis=-1))
    inter = jnp.exp(g - m_t)
    qk = jnp.einsum('bhcld,bhcsd->bhcls', qc, kc) * jnp.exp(Dm - m_t[..., None])
    num = inter[..., None] * jnp.einsum('bhcld,bhcde->bhcle', qc, Cp) + jnp.einsum('bhcls,bhcse->bhcle', qk, vc)
    den = inter * jnp.einsum('bhcld,bhcd->bhcl', qc, Np) + jnp.sum(qk, axis=-1)
    h = num / jnp.maximum(jnp.abs(den), jnp.exp(-m_t))[..., None]
    h = jnp.moveaxis(h, 1, 3).reshape(B, S, MLSTM_WIDTH)
    return h

def even_layer(x, norm_g, w_in, conv_w, pool_w, pool_scale, w_out):
    h = rmsnorm(x, norm_g)
    xa, bg, cg, gate_a, u, gate_b = split_cols(h @ w_in, EVEN_SIZES)
    ya = short_conv_mixer(xa, bg, cg, conv_w) * jax.nn.silu(gate_a)
    yb = pool_mixer(u, pool_w, pool_scale) * jax.nn.silu(gate_b)
    return x + jnp.concatenate([ya, yb], axis=-1) @ w_out

def odd_layer(x, norm_g, w_in, i_bias, f_bias, sinks, w_out):
    B, S = x.shape[0], x.shape[1]
    h = rmsnorm(x, norm_g)
    (cq, ck, cv, gate_c, dq, dk, dv, di, df, do, gate_d) = split_cols(h @ w_in, ODD_SIZES)
    att = sliding_window_attention(
        cq.reshape(B, S, ATT_HEADS, ATT_HEAD_DIM),
        ck.reshape(B, S, ATT_KV_HEADS, ATT_HEAD_DIM),
        cv.reshape(B, S, ATT_KV_HEADS, ATT_HEAD_DIM), sinks)
    yc = att * jax.nn.silu(gate_c)
    mem = mlstm(dq.reshape(B, S, MLSTM_HEADS, MLSTM_QK_DIM),
                dk.reshape(B, S, MLSTM_HEADS, MLSTM_QK_DIM),
                dv.reshape(B, S, MLSTM_HEADS, MLSTM_V_DIM),
                di.astype(jnp.float32) + i_bias.astype(jnp.float32),
                df.astype(jnp.float32) + f_bias.astype(jnp.float32))
    yd = (mem * jax.nn.sigmoid(do.astype(jnp.float32))).astype(x.dtype) * jax.nn.silu(gate_d)
    return x + jnp.concatenate([yc, yd], axis=-1) @ w_out

def setup_inputs(seed: int = 0) -> dict:
    key = jax.random.key(seed)
    ks = jax.random.split(key, 16)
    nrm = jax.random.normal
    D = D_MODEL
    return {
        "x": nrm(ks[0], (BATCH, SEQ, D), jnp.float32),
        "even_norm": 1.0 + 0.02 * nrm(ks[1], (N_EVEN, D), jnp.float32),
        "even_w_in": nrm(ks[2], (N_EVEN, D, EVEN_IN), jnp.float32) * D ** -0.5,
        "even_conv_w": nrm(ks[3], (N_EVEN, CONV_K, CONV_WIDTH), jnp.float32) * CONV_K ** -0.5,
        "even_pool_w": nrm(ks[4], (N_EVEN, len(POOL_WINDOWS), POOL_GROUP, POOL_GROUP), jnp.float32) * POOL_GROUP ** -0.5,
        "even_pool_scale": 1.0 + 0.02 * nrm(ks[5], (N_EVEN, POOL_WIDTH), jnp.float32),
        "even_w_out": nrm(ks[6], (N_EVEN, EVEN_OUT, D), jnp.float32) * EVEN_OUT ** -0.5,
        "odd_norm": 1.0 + 0.02 * nrm(ks[7], (N_ODD, D), jnp.float32),
        "odd_w_in": nrm(ks[8], (N_ODD, D, ODD_IN), jnp.float32) * D ** -0.5,
        "odd_i_bias": 0.1 * nrm(ks[9], (N_ODD, MLSTM_HEADS), jnp.float32),
        "odd_f_bias": 3.0 + 0.1 * nrm(ks[10], (N_ODD, MLSTM_HEADS), jnp.float32),
        "odd_sinks": 0.1 * nrm(ks[11], (N_ODD, ATT_HEADS), jnp.float32),
        "odd_w_out": nrm(ks[12], (N_ODD, ODD_OUT, D), jnp.float32) * ODD_OUT ** -0.5,
        "final_norm": 1.0 + 0.02 * nrm(ks[13], (D,), jnp.float32),
    }

def reference(x, even_norm, even_w_in, even_conv_w, even_pool_w, even_pool_scale, even_w_out,
              odd_norm, odd_w_in, odd_i_bias, odd_f_bias, odd_sinks, odd_w_out, final_norm):
    for layer in range(DEPTH):
        j = layer // 2
        if layer % 2 == 0:
            x = even_layer(x, even_norm[j], even_w_in[j], even_conv_w[j], even_pool_w[j],
                           even_pool_scale[j], even_w_out[j])
        else:
            x = odd_layer(x, odd_norm[j], odd_w_in[j], odd_i_bias[j], odd_f_bias[j],
                          odd_sinks[j], odd_w_out[j])
    return rmsnorm(x, final_norm)


_drawn_inputs = setup_inputs


def setup_inputs(seed=0):
    import zlib

    import numpy as np

    out = dict(_drawn_inputs(seed))
    spreads = {}
    factors = {'even_pool_scale': 3.672, 'odd_i_bias': 4.489, 'odd_sinks': 53.5, 'final_norm': 7.532}
    for name, (base, spread) in spreads.items():
        noise = np.random.default_rng([zlib.crc32(name.encode()), seed]).standard_normal(out[name].shape)
        drawn = base * np.exp(spread * noise) if base else spread * noise
        out[name] = __import__('jax').numpy.asarray(drawn.astype(out[name].dtype))
    for name, factor in factors.items():
        out[name] = (out[name] * factor).astype(out[name].dtype)
    return out
```

```python
from contextlib import ExitStack

import concourse.bass as bass
from concourse import mybir

F32 = mybir.dt.float32
F32R = mybir.dt.float32r
I32 = mybir.dt.int32
ALU = mybir.AluOpType
ACT = mybir.ActivationFunctionType
AX = mybir.AxisListType

P = 128
D = 1024
S = 2048
TB = 512
NB = S // TB
TT = TB // P
KT = D // P
HALF = D // 2
CONV = 512
GROUPS = 4
HEADS, KVH, HD = 8, 2, 64
MH, MD, ME = 4, 64, 128
EPS = 1e-6
MASKED = -1e30
QSCALE = 0.125
RSQRT_MAGIC = float(0x5F3759DF)

E_XA, E_BG, E_CG, E_GA, E_U, E_GB = (CONV * i for i in range(6))
O_CQ, O_CK, O_CV, O_GC, O_DQ, O_DK, O_DV, O_DI, O_DO = 0, 512, 640, 768, 1280, 1536, 1792, 2304, 2312
O_GD = O_DO + 512

U_CONV, U_POOL, U_EOUT = 0, 16, 24
U_DK, U_DV, U_DQ, U_CK, U_CV, U_CQ, U_DOGD, U_GC, U_OOUT = 32, 34, 38, 40, 41, 42, 46, 54, 58
UNITS = 66
STAGES, SLOTS = 3, 2
OOUT_ORDER = (2, 3, 0, 1)
PIECES = 2 * TT

POOL_SETUP = 69
CONSTS = 10
DVE_STEPS = 319


def trunk(nc, x, even_norm, even_w_in, even_conv_w, even_pool_w, even_pool_scale, even_w_out,
          odd_norm, odd_w_in, odd_i_bias, odd_f_bias, odd_sinks, odd_w_out, final_norm, out):
    ew, ow = even_w_in[0], odd_w_in[0]
    ewo, owo = even_w_out[0], odd_w_out[0]
    rows_dram = nc.dram_tensor("gate_rows", [MH, 3, TB], F32, kind="Internal").ap()

    def chan_unit(w, col):
        return [(slice(0, P), w[:, col:col + P].rearrange("(k p) c -> p k c", p=P), None)]

    def head_pair_unit(w, col, j):
        return [(slice(0, P), w[:, col + 256 * g + 64 * j:col + 256 * g + 64 * j + 64]
                 .rearrange("(k p) c -> p k c", p=P), g) for g in range(KVH)]

    def row_unit(w, row, col):
        return [(slice(0, P), w[row:row + 2 * P, col:col + 512].rearrange("(k p) c -> p k c", p=P), "rows")]

    def head_row_unit(w, kp, col):
        return [(slice(64 * g, 64 * g + 64),
                 w[256 * g + 128 * kp:256 * g + 128 * kp + 128, col:col + 512]
                 .rearrange("(k p) c -> p k c", p=64), "rows") for g in range(KVH)]

    units = []
    for c in range(4):
        units += [chan_unit(ew, o + P * c) for o in (E_CG, E_XA, E_BG, E_GA)]
    for g in range(GROUPS):
        units += [chan_unit(ew, o + P * g) for o in (E_U, E_GB)]
    units += [row_unit(ewo, 256 * kp, 512 * n) for n in range(2) for kp in range(4)]
    units += [chan_unit(ow, O_DK + P * i) for i in range(2)]
    units += [row_unit(ow, 256 * kp, O_DV) for kp in range(4)]
    units += [chan_unit(ow, O_DQ + P * i) for i in range(2)]
    units += [chan_unit(ow, O_CK), chan_unit(ow, O_CV)]
    units += [head_pair_unit(ow, O_CQ, j) for j in range(4)]
    for j in range(4):
        units += [chan_unit(ow, O_DO + P * j), chan_unit(ow, O_GD + P * j)]
    units += [head_pair_unit(ow, O_GC, j) for j in range(4)]
    for n in range(2):
        for kp in OOUT_ORDER:
            units.append(head_row_unit(owo, kp, 512 * n) if kp < 2 else row_unit(owo, 256 * kp, 512 * n))
    assert len(units) == UNITS and UNITS % STAGES == 0 and UNITS % SLOTS == 0
    stage_total = [16 * sum(len(units[i]) for i in range(s, UNITS, STAGES)) for s in range(STAGES)]
    stage_upto = [16 * sum(len(units[j]) for j in range(i % STAGES, i + 1, STAGES)) for i in range(UNITS)]

    ctx = ExitStack()
    with ctx:
        def sb(name, shape, dt=F32):
            return ctx.enter_context(nc.sbuf_tensor(name, shape, dt))

        def sem(name):
            return ctx.enter_context(nc.semaphore(name))

        stage = [sb(f"stage{i}", [P, KT * P]) for i in range(STAGES)]
        w_hi = [sb(f"w_hi{i}", [P, KT * P], F32R) for i in range(SLOTS)]
        w_lo = [sb(f"w_lo{i}", [P, KT * P], F32R) for i in range(SLOTS)]
        h_hi = sb("h_hi", [P, KT, TB], F32R)
        h_lo = sb("h_lo", [P, KT, TB], F32R)
        y_hi = sb("y_hi", [P, KT, TB], F32R)
        y_lo = sb("y_lo", [P, KT, TB], F32R)
        xin = sb("xin", [P, TT, D])
        mixed = xin[:, :, :].rearrange("p t d -> p (t d)").rearrange("p (k t) -> p k t", k=KT)
        gate_rows = mixed[0:MH, 0:4, :]
        res = sb("res", [P, TT, D])
        gains = [sb(f"gain{i}", [P, D]) for i in range(3)]
        proj = sb("proj", [P, 12 * TB])
        q_att = proj[:, 0:4 * TB].rearrange("p (j t) -> p j t", j=4)
        q_mem = proj[:, 4 * TB:6 * TB].rearrange("p (j t) -> p j t", j=2)
        k_mem = proj[:, 6 * TB:8 * TB].rearrange("p (j t) -> p j t", j=2)
        v_mem = proj[:, 8 * TB:12 * TB].rearrange("p (c e) -> p c e", c=TT)
        PW = TB + 16
        conv_u = [proj[:, 5 * PW * i:5 * PW * i + 2 + TB] for i in range(2)]
        conv_y = [proj[:, 5 * PW * i + PW:5 * PW * i + PW + TB] for i in range(2)]
        conv_c = [proj[:, 5 * PW * i + 2 * PW:5 * PW * i + 2 * PW + TB] for i in range(2)]
        conv_t = [proj[:, 5 * PW * i + 3 * PW:5 * PW * i + 3 * PW + TB] for i in range(2)]
        conv_g = [proj[:, 5 * PW * i + 4 * PW:5 * PW * i + 4 * PW + TB] for i in range(2)]
        pool_u = [proj[:, 5 * PW * i:5 * PW * i + PW] for i in range(2)]
        pool_t = [proj[:, 5 * PW * i + PW:5 * PW * i + 2 * PW] for i in range(2)]
        pool_g = [proj[:, 5 * PW * i + 2 * PW:5 * PW * i + 3 * PW] for i in range(2)]
        pool_s = [proj[:, 5 * PW * i + 3 * PW:5 * PW * i + 4 * PW] for i in range(2)]
        pool_d = [proj[:, 5 * PW * i + 4 * PW:5 * PW * i + 5 * PW] for i in range(2)]
        pool_diff = [(pool_s, pool_d)[(g + 1) % 2][g % 2] for g in range(GROUPS)]
        work = sb("work", [P, 8 * TB])
        xs = [work[:, D * i:D * i + D] for i in range(2)]
        scores = work[:, 0:4 * TB].rearrange("p (i k) -> p i k", i=8)
        probs_t = work[:, 4 * TB:8 * TB].rearrange("p (i b n) -> p i b n", i=2, b=2)
        row_bc = [work[:, 5 * 256 * i:5 * 256 * i + 4 * P].rearrange("p (h t) -> p h t", h=MH) for i in range(2)]
        emt_bc = [work[:, 5 * 256 * i + 512:5 * 256 * i + 1024].rearrange("p (h t) -> p h t", h=MH) for i in range(2)]
        inter_bc = [work[:, 5 * 256 * i + 1024:5 * 256 * i + 1280].rearrange("p (h t) -> p h t", h=2) for i in range(2)]
        decay_w = work[:, 2560:3072].rearrange("p (h t) -> p h t", h=MH)
        k_wr = work[:, 3328:3584].rearrange("p (h t) -> p h t", h=MH)
        recip = work[:, 3584:4096].rearrange("p (h t) -> p h t", h=MH)
        q_plain = sb("q_plain", [P, MH, P])
        q_inter = sb("q_inter", [P, MH, P])
        k_att = sb("k_att", [P, P + TB])
        v_att = sb("v_att", [P, TT + 1, P])
        state = sb("state", [P, 2, 2 * ME])
        bias = sb("bias", [P, HEADS, 2 * P])
        causal = sb("causal", [P, P])
        ident = sb("ident", [P, P])
        ones = sb("ones", [P, P])
        conv_hist = sb("conv_hist", [P, 4, 2])
        pool_hist = sb("pool_hist", [P, GROUPS, 16])
        pool_w = sb("pool_w", [P, GROUPS, P])
        conv_w = sb("conv_w", [P, 3, 4])
        pool_sc = sb("pool_sc", [P, GROUPS])
        corr = sb("corr", [P, GROUPS, 16])
        first = sb("first", [P, 1])
        neg_sink = sb("neg_sink", [P, HEADS])
        wg_raw = sb("wg_raw", [P, KT, 2 * MH])
        wg_hi = sb("wg_hi", [P, KT, 2 * MH], F32R)
        wg_lo = sb("wg_lo", [P, KT, 2 * MH], F32R)
        gates_tok = sb("gates_tok", [P, TT, 2 * MH])
        ib = sb("ib", [MH, 1])
        fb = sb("fb", [MH, 1])
        chunk_mask = sb("chunk_mask", [MH, TB])
        row_u = sb("row_u", [MH, TB])
        row_t = mixed[0:MH, 4, :]
        row_c = mixed[0:MH, 5, :]
        row_m = mixed[0:MH, 6, :]
        m_prev = sb("m_prev", [MH, TT])
        carry_m = sb("carry_m", [MH, 1])
        carry_b = sb("carry_b", [MH, 1])
        cols = sb("cols", [P, 2, 2 * MH])
        sums = sb("sums", [P, 3, TT, 2])
        rs = sb("rs", [P, TT, 5])
        sm = sb("sm", [P, 2, 24])
        junk = sb("junk", [P, HALF])
        cv_chan = junk[:, :]
        gate_tanh = [proj[:, (4 + i) * TB:(5 + i) * TB] for i in range(2)]
        gate_a, gate_b = proj[:, 6 * TB:7 * TB], proj[:, 7 * TB:8 * TB]
        att_gate = proj[:, 8 * TB:12 * TB].rearrange("p (j t) -> p j t", j=4)

        bank = [ctx.enter_context(nc.psum_tensor(f"bank{i}", [P, 512], F32)) for i in range(2)]
        pair_a = ctx.enter_context(nc.psum_tensor("pair_a", [P, 2, 512], F32))
        pair_b = ctx.enter_context(nc.psum_tensor("pair_b", [P, 2, 512], F32))
        pair_c = ctx.enter_context(nc.psum_tensor("pair_c", [P, 2, 512], F32))
        banks = [bank[0][:, :], bank[1][:, :], pair_a[:, 0, :], pair_a[:, 1, :],
                 pair_b[:, 0, :], pair_b[:, 1, :], pair_c[:, 0, :], pair_c[:, 1, :]]

        s_staged = [sem(f"staged{i}") for i in range(STAGES)]
        s_split = sem("split")
        s_slot = sem("slot_free")
        s_unit = sem("unit_done")
        s_x = [sem(f"x_in{i}") for i in range(TT)]
        s_const = sem("consts")
        s_pool = sem("pool_setup")
        s_vset = sem("vec_setup")
        s_sq = sem("squares")
        s_xs = sem("scaled")
        s_xt = sem("transposed")
        s_hhi = sem("h_hi_ready")
        s_hlo = sem("h_lo_ready")
        s_dve = sem("dve_step")
        s_whi = sem("whi")
        s_conv_c = sem("conv_c")
        s_conv_t = sem("conv_t")
        s_pool_u = sem("pool_u")
        s_pool_t = sem("pool_t")
        s_pool_diff = sem("pool_diff")
        s_pool_gate = sem("pool_gate")
        s_gates_tok = sem("gates_tok")
        s_row_abs = sem("row_abs")
        s_row_exp = sem("row_exp")
        s_row_ln = sem("row_ln")
        s_rows_end = sem("rows_end")
        s_rows_exp = sem("rows_exp")
        s_k_mem = sem("k_mem")
        s_v_mem = sem("v_mem")
        s_q_mem = sem("q_mem")
        s_k_att = sem("k_att")
        s_hist = sem("hist")
        s_q_plain = sem("q_plain")
        s_cv_chan = sem("cv_chan")
        s_q_att = sem("q_att")
        s_v_att = sem("v_att")
        s_mem_masked = sem("mem_masked")
        s_mem_exp = sem("mem_exp")
        s_mem_scored = sem("mem_scored")
        s_mem_abs = sem("mem_abs")
        s_mem_state = sem("mem_state")
        s_mem_end = sem("mem_end")
        s_att_added = sem("att_added")
        s_att_max = sem("att_max")
        s_att_exp = sem("att_exp")
        s_att_normed = sem("att_normed")
        s_att_pa = sem("att_pa")
        s_att_pv = sem("att_pv")
        s_att_out = sem("att_out")
        s_gate_t = sem("gate_t")
        s_gated = sem("gated")
        s_ye = sem("y_even_ready")
        s_yo = sem("y_odd_ready")
        s_pm = sem("pool_product")
        s_res = sem("res_ready")
        s_fin = sem("fin_ready")
        s_norm = sem("out_normed")
        s_store = [sem(f"stored{i}") for i in range(TT)]
        s_gmm = sem("gates_product")
        s_grow = sem("gates_rows")
        s_rowst = sem("rows_stored")
        s_bc = [sem(f"rows_bc{i}") for i in range(2)]
        s_cvt = sem("values_transposed")
        s_ma = sem("mem_scores")
        s_mb = sem("mem_products")
        s_aa = sem("att_scores")
        s_ab = sem("att_transposed")
        s_ac = sem("att_values")
        block = ctx.enter_context(nc.Block())

        def wait_unit(eng, b, u):
            eng.wait_ge(s_unit, b * UNITS + u + 1 + SLOTS)

        @block.sync
        def _(sp):
            def load_unit(i):
                for parts, src, kind in units[i]:
                    dst = stage[i % STAGES]
                    if kind == "rows":
                        d = dst[parts, :].rearrange("p (k c) -> p k c", k=2)
                    else:
                        d = dst[parts, :].rearrange("p (k c) -> p k c", k=KT)
                        if kind is not None:
                            d = d[:, :, 64 * kind:64 * kind + 64]
                    sp.dma_start(d, src).then_inc(s_staged[i % STAGES], 16)

            x_rows = x[0]
            with sp.Fori(0, NB) as b:
                sp.wait_ge(s_yo, b * 8 + 1)
                for tt in range(TT):
                    sp.dma_start(xin[:, tt, :], x_rows[bass.ds(b * TB + tt * P, P), :]).then_inc(s_x[tt], 16)
                for i in range(UNITS):
                    sp.wait_ge(s_split, b * UNITS + i + 1)
                    load_unit(i)
                    if i in (U_CK, U_CK + 3, U_CK + 5):
                        for c in {U_CK: (0, 1), U_CK + 3: (2,), U_CK + 5: (3,)}[i]:
                            if c == 0:
                                sp.wait_ge(s_rowst, b * 32 + 32)
                            if c >= 2:
                                sp.wait_ge(s_mem_end, b * 4 + c - 1)
                            r = rows_dram[:, :, c * P:(c + 1) * P]
                            sp.dma_start(row_bc[c % 2], r[:, 2, :].partition_broadcast(P)).then_inc(s_bc[c % 2], 16)
                            sp.dma_start(emt_bc[c % 2], r[:, 1, :].partition_broadcast(P)).then_inc(s_bc[c % 2], 16)
                            for g in range(2):
                                sp.dma_start(inter_bc[c % 2][64 * g:64 * g + 64],
                                             r[g:MH:2, 0, :].partition_broadcast(64)).then_inc(s_bc[c % 2], 16)

        @block.gpsimd
        def _(pool):
            g = nc.gpsimd
            n = [0]

            def step(ins):
                n[0] += 1
                ins.then_inc(s_pool, 1)
                pool.wait_ge(s_pool, n[0])

            step(g.memset(ident[:, :], 0.0))
            step(g.affine_select(out=ident[:, :], in_=ident[:, :], compare_op=ALU.not_equal, fill=1.0,
                                 base=0, pattern=[[-1, P]], channel_multiplier=1))
            step(g.memset(causal[:, :], 0.0))
            step(g.affine_select(out=causal[:, :], in_=causal[:, :], compare_op=ALU.is_ge, fill=MASKED,
                                 base=0, pattern=[[1, P]], channel_multiplier=-1))
            step(g.memset(ones[:, :], 1.0))
            step(g.iota(junk[:, 0:2 * P], pattern=[[-1, 2 * P]], base=P, channel_multiplier=1,
                        allow_small_or_imprecise_dtypes=True))
            for h in range(HEADS):
                step(g.tensor_scalar(bias[:, h, :], junk[:, 0:2 * P], -2.0 ** (-8.0 * (h + 1) / HEADS), 0.0,
                                     ALU.mult, ALU.add))
                step(g.affine_select(out=bias[:, h, :], in_=bias[:, h, :], compare_op=ALU.is_ge, fill=MASKED,
                                     base=P, pattern=[[-1, 2 * P]], channel_multiplier=1))
                step(g.affine_select(out=bias[:, h, :], in_=bias[:, h, :], compare_op=ALU.is_gt, fill=MASKED,
                                     base=0, pattern=[[1, 2 * P]], channel_multiplier=-1))
            for t in (q_plain[:, :, :], q_inter[:, :, :], k_att[:, :], v_att[:, :, :], state[:, :, :], conv_hist[:, :, :], pool_hist[:, :, :],
                      carry_m[:, :], carry_b[:, :]):
                step(g.memset(t, 0.0))
            step(g.memset(first[:, :], MASKED))
            step(g.memset(chunk_mask[:, :], 1.0))
            step(g.memset(chunk_mask[:, 0:TB:P], 0.0))
            step(g.memset(corr[:, :, :], 1.0))
            for k in range(GROUPS):
                w = 2 << k
                for t in range(w - 1):
                    step(g.memset(corr[:, k, t:t + 1], w / (t + 1.0)))
            assert n[0] == POOL_SETUP, n[0]
            pool.wait_ge(s_const, 16 * CONSTS)
            g.tensor_scalar(wg_hi[:, :, :], wg_raw[:, :, :], 1.0, 0.0, ALU.mult, ALU.add).then_inc(s_pool, 1)
            pool.wait_ge(s_pool, POOL_SETUP + 1)
            g.tensor_tensor(wg_lo[:, :, :], wg_raw[:, :, :], wg_hi[:, :, :].bitcast(F32), ALU.subtract).then_inc(s_pool, 1)
            pool.wait_ge(s_pool, POOL_SETUP + 2)
            g.sem_inc(s_split, STAGES)
            with pool.Fori(0, NB) as b:
                for i in range(UNITS):
                    sg, sl = i % STAGES, i % SLOTS
                    pool.wait_ge(s_staged[sg], b * stage_total[sg] + stage_upto[i])
                    pool.wait_ge(s_unit, b * UNITS + i + 1)
                    g.sem_inc(s_slot)
                    g.tensor_scalar(w_hi[sl][:, :], stage[sg][:, :], 1.0, 0.0, ALU.mult, ALU.add).then_inc(s_whi, 1)
                    pool.wait_ge(s_whi, b * UNITS + i + 1)
                    g.tensor_tensor(w_lo[sl][:, :], stage[sg][:, :], w_hi[sl][:, :].bitcast(F32),
                                    ALU.subtract).then_inc(s_split, 1)

        @block.tensor
        def _(pe):
            t = nc.tensor

            def mm3(dst, l_hi, l_lo, r_hi, r_lo, start, stop):
                t.matmul(dst, l_hi, r_hi, start=start, stop=False)
                t.matmul(dst, l_hi, r_lo, start=False, stop=False)
                return t.matmul(dst, l_lo, r_hi, start=False, stop=stop)

            pe.wait_ge(s_pool, POOL_SETUP + 2)
            pe.wait_ge(s_const, 16 * CONSTS)
            pe.sem_inc(s_unit, SLOTS)
            with pe.Fori(0, NB) as b:
                def chan(u, dst):
                    pe.wait_ge(s_split, b * UNITS + u + 1 + STAGES)
                    sl = u % SLOTS
                    for k in range(KT):
                        last = mm3(dst, w_hi[sl][:, k * P:(k + 1) * P], w_lo[sl][:, k * P:(k + 1) * P],
                                   h_hi[:, k, :], h_lo[:, k, :], k == 0, k == KT - 1)
                    last.then_inc(s_unit, 1)

                def token(u, kp, src_hi, src_lo, base, start, stop):
                    pe.wait_ge(s_split, b * UNITS + u + 1 + STAGES)
                    sl = u % SLOTS
                    for kk in range(2):
                        k = 2 * kp + kk
                        for tt in range(TT):
                            a = slice(tt * P, (tt + 1) * P)
                            c = slice(512 * kk, 512 * kk + 512)
                            last = mm3(banks[base + tt], src_hi[:, k, a], src_lo[:, k, a],
                                       w_hi[sl][:, c], w_lo[sl][:, c], start and kk == 0, stop and kk == 1)
                    last.then_inc(s_unit, 1)

                def norm_transposes(ph):
                    for tt in range(TT):
                        pe.wait_ge(s_xs, b * 8 + 4 * ph + tt + 1)
                        for hb in range(2):
                            if tt >= 2:
                                pe.wait_ge(s_hlo, b * 16 + 8 * ph + 2 * (tt - 2) + hb + 1)
                            for q in range(4):
                                k = 4 * hb + q
                                last = t.transpose(banks[2 * (tt % 2) + hb][:, q * P:(q + 1) * P],
                                                   xs[tt % 2][:, k * P:(k + 1) * P], ident[:, :])
                            last.then_inc(s_xt, 1)

                norm_transposes(0)
                pe.wait_ge(s_hlo, b * 16 + 8)
                for c in range(4):
                    for j in range(4):
                        if c >= 2 and j == 0:
                            pe.wait_ge(s_ye, b * 8 + c - 1)
                        chan(U_CONV + 4 * c + j, banks[4 * (c % 2) + j])

                def pool_product(g):
                    pe.wait_ge(s_pool_diff, b * 4 + g + 1)
                    t.matmul(banks[4 + g], pool_w[:, g, :], pool_diff[g][:, 16:PW], start=True, stop=True
                             ).then_inc(s_pm, 1)

                for g in range(GROUPS):
                    if g == 0:
                        pe.wait_ge(s_ye, b * 8 + 3)
                    if g >= 2:
                        pe.wait_ge(s_pool_gate, b * 4 + g - 1)
                    for j in range(2):
                        chan(U_POOL + 2 * g + j, banks[2 * (g % 2) + j])
                    if g == 1:
                        pe.wait_ge(s_ye, b * 8 + 4)
                    if g >= 1:
                        pool_product(g - 1)
                pe.wait_ge(s_pool_gate, b * 4 + 4)
                for n in range(2):
                    for kp in range(4):
                        if n == 0 and kp == 2:
                            pool_product(3)
                            pe.wait_ge(s_ye, b * 8 + 8)
                        token(U_EOUT + 4 * n + kp, kp, y_hi, y_lo, 4 * n, kp == 0, kp == 3)
                pe.wait_ge(s_res, b * 8 + 4)
                norm_transposes(1)
                pe.wait_ge(s_hlo, b * 16 + 16)
                for tt in range(TT):
                    for k in range(KT):
                        a = slice(tt * P, (tt + 1) * P)
                        last = mm3(banks[2][:, 8 * tt:8 * tt + 8], h_hi[:, k, a], h_lo[:, k, a],
                                   wg_hi[:, k, :], wg_lo[:, k, :], k == 0, k == KT - 1)
                last.then_inc(s_gmm, 1)
                chan(U_DK, banks[0])
                pe.wait_ge(s_gates_tok, b + 1)
                for j in range(2):
                    for tt in range(TT):
                        last = t.transpose(banks[2 + j][0:MH, tt * P:(tt + 1) * P],
                                           gates_tok[:, tt, MH * j:MH * j + MH], ident[:, :])
                last.then_inc(s_grow, 1)
                chan(U_DK + 1, banks[1])
                for kp in range(4):
                    token(U_DV + kp, kp, h_hi, h_lo, 4, kp == 0, kp == 3)

                def mem_a(c):
                    pe.wait_ge(s_q_plain, b * 4 + c + 1)
                    a = slice(c * P, (c + 1) * P)
                    if c == 0:
                        pe.wait_ge(s_v_mem, b * 4 + 4)
                        pe.wait_ge(s_q_mem, b * 2 + 2)
                        pe.wait_ge(s_rows_exp, b + 1)
                        pe.wait_ge(s_rows_end, b + 1)
                    else:
                        pe.wait_ge(s_mem_scored, b * 4 + c)
                    for i in range(2):
                        t.transpose(banks[5][:, i * P:(i + 1) * P], k_mem[:, i, a], ident[:, :])
                    t.transpose(banks[5][:, 256:260], row_u[:, a], ident[0:MH, 0:MH])
                    t.transpose(banks[5][:, 260:264], gate_rows[:, 2, a], ident[0:MH, 0:MH])
                    for h in range(MH):
                        last = t.matmul(banks[4][:, h * P:(h + 1) * P], k_mem[:, h // 2, a],
                                        q_plain[:, h, :], start=True, stop=True)
                    last.then_inc(s_ma, 1)

                def mem_b(c):
                    pe.wait_ge(s_mem_scored, b * 4 + c + 1)
                    if c:
                        pe.wait_ge(s_mem_state, b * 4 + c)
                        pe.wait_ge(s_mem_end, b * 4 + c)
                    for h in range(MH):
                        hs = slice(h * P, (h + 1) * P)
                        t.matmul(banks[6][:, hs], v_mem[:, c, hs], decay_w[:, h, :], start=True, stop=False)
                        t.matmul(banks[6][:, hs], state[:, h // 2, 0:ME], q_inter[:, h, :], start=False, stop=True)
                    for h in range(MH):
                        hs = slice(h * P, (h + 1) * P)
                        t.matmul(banks[7][:, hs], ones[:, :], decay_w[:, h, :], start=True, stop=False)
                        t.matmul(banks[7][:, hs], state[:, h // 2, ME:2 * ME], q_inter[:, h, :], start=False, stop=True)
                    for h in range(MH):
                        r = slice(64 * (h % 2), 64 * (h % 2) + 64)
                        o = 256 * (h // 2)
                        t.matmul(banks[3][r, o:o + ME], k_wr[:, h, :], v_mem[:, c, h * P:(h + 1) * P],
                                 start=True, stop=True)
                        last = t.matmul(banks[3][r, o + ME:o + 2 * ME], k_wr[:, h, :], ones[:, :],
                                        start=True, stop=True)
                    last.then_inc(s_mb, 1)

                pe.wait_ge(s_k_mem, b * 2 + 2)
                chan(U_DQ, banks[0])
                chan(U_DQ + 1, banks[1])
                pe.wait_ge(s_q_mem, b * 2 + 1)
                chan(U_CK, banks[0])
                mem_a(0)
                pe.wait_ge(s_q_mem, b * 2 + 2)
                chan(U_CV, banks[1])
                mem_b(0)
                mem_a(1)
                pe.wait_ge(s_k_att, b + 1)
                chan(U_CQ, banks[0])
                pe.wait_ge(s_cv_chan, b + 1)
                for tt in range(TT):
                    last = t.transpose(banks[2][:, tt * P:(tt + 1) * P], cv_chan[:, tt * P:(tt + 1) * P], ident[:, :])
                last.then_inc(s_cvt, 1)
                mem_b(1)
                mem_a(2)
                chan(U_CQ + 1, banks[1])
                mem_b(2)
                mem_a(3)
                pe.wait_ge(s_q_att, b * 4 + 1)
                chan(U_CQ + 2, banks[0])
                mem_b(3)
                pe.wait_ge(s_q_att, b * 4 + 2)
                chan(U_CQ + 3, banks[1])
                pe.wait_ge(s_q_att, b * 4 + 4)
                pe.wait_ge(s_v_att, b + 1)

                def att_a(p):
                    sbk, g = p // 2, p % 2
                    r = slice(64 * g, 64 * g + 64)
                    if p:
                        pe.wait_ge(s_att_added, b * 8 + p)
                    else:
                        pe.wait_ge(s_mem_end, b * 4 + 4)
                    for j in range(4):
                        last = t.matmul(pair_b[:, j // 2, 256 * (j % 2):256 * (j % 2) + 256],
                                        q_att[r, j, sbk * P:(sbk + 1) * P], k_att[r, sbk * P:(sbk + 2) * P],
                                        start=True, stop=True)
                    last.then_inc(s_aa, 1)

                def att_b(p):
                    pe.wait_ge(s_att_normed, b * 8 + p + 1)
                    if p:
                        pe.wait_ge(s_att_pa, b * 8 + p)
                        pe.wait_ge(s_att_pv, b * 8 + p)
                    for kb in range(2):
                        for j in range(4):
                            last = t.transpose(pair_c[:, kb, j * P:(j + 1) * P],
                                               scores[:, 4 * (p % 2) + j, kb * P:(kb + 1) * P], ident[:, :])
                    last.then_inc(s_ab, 1)

                def att_c(p):
                    sbk, g = p // 2, p % 2
                    pe.wait_ge(s_att_pa, b * 8 + p + 1)
                    pe.wait_ge(s_att_pv, b * 8 + p + 1)
                    if sbk >= 2 and g == 0:
                        pe.wait_ge(s_att_out, b * 4 + sbk - 1)
                    elif g == 0 and sbk == 1:
                        pe.wait_ge(s_mem_state, b * 4 + 4)
                    for kb in range(2):
                        last = t.matmul(banks[2 + sbk % 2][64 * g:64 * g + 64, :],
                                        v_att[:, sbk + kb, 64 * g:64 * g + 64], probs_t[:, p % 2, kb, :],
                                        start=(kb == 0), stop=(kb == 1))
                    last.then_inc(s_ac, 1)

                for s in range(12):
                    if 2 <= s < PIECES + 2:
                        att_b(s - 2)
                    if 3 <= s < PIECES + 3:
                        att_c(s - 3)
                    if s < PIECES:
                        att_a(s)
                    if s in (2, 4, 6, 8):
                        pe.wait_ge(s_gate_t, b * 12 + s - 1)
                    elif s > 1:
                        pe.wait_ge(s_gated, b * 8 + (s - 1) // 2 if s < 10 else b * 8 + s - 5)
                    chan(U_DOGD + s, banks[s % 2])
                for n in range(2):
                    for i, kp in enumerate(OOUT_ORDER):
                        if n == 0 and i == 0:
                            pe.wait_ge(s_yo, b * 8 + 4 + 1)
                            pe.wait_ge(s_gated, b * 8 + 8)
                            pe.wait_ge(s_att_out, b * 4 + 4)
                        if n == 0 and i == 2:
                            pe.wait_ge(s_yo, b * 8 + 8 + 1)
                        token(U_OOUT + 4 * n + i, kp, y_hi, y_lo, 4 * n, i == 0, i == 3)

        @block.scalar
        def _(act):
            a = nc.scalar
            for dst, src in (
                    (gains[0][:, :], even_norm[0].partition_broadcast(P)),
                    (gains[1][:, :], odd_norm[0].partition_broadcast(P)),
                    (gains[2][:, :], final_norm.partition_broadcast(P)),
                    (pool_w[:, :, :], even_pool_w[0].rearrange("g c d -> c g d")),
                    (conv_w[:, :, :], even_conv_w[0].rearrange("k (c p) -> p k c", p=P)),
                    (pool_sc[:, :], even_pool_scale[0].rearrange("(g p) -> p g", p=P)),
                    (neg_sink[:, :], odd_sinks[0].partition_broadcast(P)),
                    (wg_raw[:, :, :], ow[:, O_DI:O_DI + 2 * MH].rearrange("(k p) c -> p k c", p=P)),
                    (ib[:, :], odd_i_bias[0].rearrange("(h o) -> h o", o=1)),
                    (fb[:, :], odd_f_bias[0].rearrange("(h o) -> h o", o=1))):
                act.dma_start(dst, src, allow_slow_non_contiguous=True).then_inc(s_const, 16)
            act.wait_ge(s_const, 16 * CONSTS)
            act.wait_ge(s_pool, POOL_SETUP)
            out_rows = out[0]
            for tt in range(TT):
                act.sem_inc(s_store[tt], 1)
            with act.Fori(0, NB) as b:
                squares = [0]

                def square(ph, src, tt, hf):
                    if squares[0]:
                        act.wait_ge(s_sq, b * 24 + squares[0])
                    squares[0] += 1
                    a.activation(junk[:, :], src[:, tt, hf * HALF:(hf + 1) * HALF], ACT.Square,
                                 accum_out=sums[:, ph, tt, hf:hf + 1]).then_inc(s_sq, 1)

                def evacuate(ph, tt):
                    for hb in range(2):
                        act.wait_ge(s_xt, b * 16 + 8 * ph + 2 * tt + hb + 1)
                        a.activation(h_hi[:, 4 * hb:4 * hb + 4, tt * P:(tt + 1) * P],
                                     banks[2 * (tt % 2) + hb].rearrange("p (k t) -> p k t", k=4),
                                     ACT.Copy).then_inc(s_hhi, 1)

                for tt in range(TT):
                    act.wait_ge(s_x[tt], b * 16 + 16)
                    square(0, xin, tt, 0)
                    square(0, xin, tt, 1)
                    if tt:
                        evacuate(0, tt - 1)
                evacuate(0, TT - 1)
                for c in range(4):
                    wait_unit(act, b, U_CONV + 4 * c)
                    if c >= 2:
                        act.wait_ge(s_ye, b * 8 + c - 1)
                    a.activation(conv_c[c % 2], banks[4 * (c % 2)], ACT.Copy).then_inc(s_conv_c, 1)
                    wait_unit(act, b, U_CONV + 4 * c + 3)
                    a.activation(conv_t[c % 2], banks[4 * (c % 2) + 3], ACT.Tanh, scale=0.5).then_inc(s_conv_t, 1)
                for g in range(GROUPS):
                    wait_unit(act, b, U_POOL + 2 * g)
                    act.wait_ge(s_ye, b * 8 + 3 + g)
                    a.activation(pool_u[g % 2][:, 16:PW], banks[2 * (g % 2)], ACT.Copy).then_inc(s_pool_u, 1)
                    wait_unit(act, b, U_POOL + 2 * g + 1)
                    a.activation(pool_t[g % 2][:, 0:TB], banks[2 * (g % 2) + 1], ACT.Tanh,
                                 scale=0.5).then_inc(s_pool_t, 1)
                for tt in range(TT):
                    act.wait_ge(s_res, b * 8 + tt + 1)
                    square(1, res, tt, 0)
                for tt in range(TT):
                    act.wait_ge(s_res, b * 8 + 4 + tt + 1)
                    square(1, res, tt, 1)
                    if tt:
                        evacuate(1, tt - 1)
                evacuate(1, TT - 1)
                act.wait_ge(s_gmm, b + 1)
                a.activation(gates_tok[:, :, :], banks[2][:, 0:8 * TT].rearrange("p (t g) -> p t g", t=TT),
                             ACT.Copy).then_inc(s_gates_tok, 1)
                wait_unit(act, b, U_DK)
                a.activation(k_mem[:, 0, :], banks[0], ACT.Copy).then_inc(s_k_mem, 1)
                act.wait_ge(s_grow, b + 1)
                a.activation(row_t[:, :], banks[3][0:MH, :], ACT.Abs, bias=fb[:, :]).then_inc(s_row_abs, 1)
                act.wait_ge(s_row_abs, b + 1)
                a.activation(row_t[:, :], row_t[:, :], ACT.Exp, scale=-1.0).then_inc(s_row_exp, 1)
                act.wait_ge(s_row_exp, b + 1)
                a.activation(row_t[:, :], row_t[:, :], ACT.Ln, bias=1.0).then_inc(s_row_ln, 1)
                wait_unit(act, b, U_DK + 1)
                a.activation(k_mem[:, 1, :], banks[1], ACT.Copy).then_inc(s_k_mem, 1)
                act.wait_ge(s_rows_end, b + 1)
                a.activation(gate_rows[:, 0:3, :], gate_rows[:, 0:3, :], ACT.Exp).then_inc(s_rows_exp, 1)
                act.wait_ge(s_rows_exp, b + 1)
                act.dma_start(rows_dram[:, 0:2, :], gate_rows[:, 0:2, :]).then_inc(s_rowst, 16)
                act.dma_start(rows_dram[:, 2, :], gate_rows[:, 3, :]).then_inc(s_rowst, 16)
                wait_unit(act, b, U_DV + 3)
                for tt in range(TT):
                    a.activation(v_mem[:, tt, :], banks[4 + tt], ACT.Copy).then_inc(s_v_mem, 1)
                for i in range(2):
                    wait_unit(act, b, U_DQ + i)
                    a.activation(q_mem[:, i, :], banks[i], ACT.Copy, scale=QSCALE).then_inc(s_q_mem, 1)

                def mem_q(c):
                    if c:
                        act.wait_ge(s_ma, b * 4 + c)
                    else:
                        act.wait_ge(s_q_mem, b * 2 + 2)
                    for g in range(2):
                        last = a.activation(q_plain[64 * g:64 * g + 64, g:MH:2, :],
                                            q_mem[64 * g:64 * g + 64, :, c * P:(c + 1) * P], ACT.Copy)
                    last.then_inc(s_q_plain, 1)

                def mem_exp(c):
                    act.wait_ge(s_mem_masked, b * 4 + c + 1)
                    if c:
                        act.wait_ge(s_mb, b * 4 + c)
                    for h in range(MH):
                        last = a.activation(decay_w[:, h, :], row_bc[c % 2][:, h, :], ACT.Exp,
                                            bias=cols[:, c % 2, h:h + 1])
                    last.then_inc(s_mem_exp, 1)
                    if c < TT - 1:
                        mem_q(c + 1)

                def mem_abs(c):
                    act.wait_ge(s_mb, b * 4 + c + 1)
                    a.activation(recip[:, :, :], banks[7].rearrange("p (h t) -> p h t", h=MH),
                                 ACT.Abs).then_inc(s_mem_abs, 1)

                def att_query(j):
                    wait_unit(act, b, U_CQ + j)
                    a.activation(q_att[:, j, :], banks[j % 2], ACT.Copy, scale=QSCALE).then_inc(s_q_att, 1)

                a.activation(k_att[:, 0:P], k_att[:, TB:TB + P], ACT.Copy).then_inc(s_hist, 1)
                a.activation(v_att[:, 0, :], v_att[:, TT, :], ACT.Copy).then_inc(s_hist, 1)
                mem_q(0)
                wait_unit(act, b, U_CK)
                act.wait_ge(s_hist, b * 2 + 2)
                a.activation(k_att[:, P:P + TB], banks[0], ACT.Copy).then_inc(s_k_att, 1)
                mem_exp(0)
                wait_unit(act, b, U_CV)
                a.activation(cv_chan[:, :], banks[1], ACT.Copy).then_inc(s_cv_chan, 1)
                mem_abs(0)
                mem_exp(1)
                att_query(0)
                act.wait_ge(s_cvt, b + 1)
                a.activation(v_att[:, 1:TT + 1, :], banks[2].rearrange("p (t c) -> p t c", t=TT),
                             ACT.Copy).then_inc(s_v_att, 1)
                mem_abs(1)
                mem_exp(2)
                att_query(1)
                mem_abs(2)
                mem_exp(3)
                att_query(2)
                mem_abs(3)
                att_query(3)

                def att_exp(p):
                    q = p % 2
                    act.wait_ge(s_att_max, b * 8 + p + 1)
                    for j in range(4):
                        a.activation(scores[:, 4 * q + j, :], scores[:, 4 * q + j, :], ACT.Exp,
                                     bias=sm[:, q, 4 + j:5 + j], accum_out=sm[:, q, 8 + j:9 + j])
                    a.activation(sm[:, q, 12:16], sm[:, q, 16:20], ACT.Exp).then_inc(s_att_exp, 1)

                for s in range(12):
                    if s < PIECES:
                        att_exp(s)
                    if 2 <= s < PIECES + 2:
                        p = s - 2
                        act.wait_ge(s_ab, b * 8 + p + 1)
                        if p >= 2:
                            act.wait_ge(s_ac, b * 8 + p - 1)
                        a.activation(probs_t[:, p % 2, 0, :], pair_c[:, 0, :], ACT.Copy).then_inc(s_att_pa, 1)
                    if s >= 4 and s % 2 == 0 and s <= 10:
                        sbk = (s - 4) // 2
                        act.wait_ge(s_ac, b * 8 + 2 * sbk + 2)
                        a.activation(mixed[:, 0:4, sbk * P:(sbk + 1) * P],
                                     banks[2 + sbk % 2].rearrange("p (j t) -> p j t", j=4),
                                     ACT.Copy).then_inc(s_att_out, 1)
                    wait_unit(act, b, U_DOGD + s)
                    if s >= 2:
                        act.wait_ge(s_gated, b * 8 + (s // 2 if s < 9 else s - 5))
                    a.activation(gate_tanh[s % 2], banks[s % 2], ACT.Tanh, scale=0.5).then_inc(s_gate_t, 1)

                for tt in range(TT):
                    act.wait_ge(s_fin, b * 8 + tt + 1)
                    square(2, res, tt, 0)
                for tt in range(TT):
                    act.wait_ge(s_fin, b * 8 + 4 + tt + 1)
                    square(2, res, tt, 1)
                for tt in range(TT):
                    act.wait_ge(s_norm, b * 4 + tt + 1)
                    act.dma_start(out_rows[bass.ds(b * TB + tt * P, P), :], res[:, tt, :]).then_inc(s_store[tt], 16)
            for tt in range(TT):
                act.wait_ge(s_store[tt], 16 * NB + 1)

        @block.vector
        def _(dve):
            v = nc.vector
            dve.wait_ge(s_const, 16 * CONSTS)
            dve.wait_ge(s_pool, POOL_SETUP)
            v.tensor_scalar(pool_sc[:, :], pool_sc[:, :], 0.5, None, ALU.mult).then_inc(s_vset, 1)
            v.tensor_scalar(neg_sink[:, :], neg_sink[:, :], -1.0, None, ALU.mult).then_inc(s_vset, 1)
            dve.sem_inc(s_yo, 1)
            dve.wait_ge(s_vset, 2)
            with dve.Fori(0, NB) as b:
                count = [0]

                def step(ins):
                    ins.then_inc(s_dve, 1)
                    count[0] += 1

                def sync():
                    dve.wait_ge(s_dve, b * DVE_STEPS + count[0])

                def link(ins):
                    step(ins)
                    sync()

                def rsqrt(ph, tt):
                    m, t, y = rs[:, tt, 0:1], rs[:, tt, 1:2], rs[:, tt, 2:3]
                    link(v.tensor_tensor(m, sums[:, ph, tt, 0:1], sums[:, ph, tt, 1:2], ALU.add))
                    link(v.tensor_scalar(m, m, 1.0 / D, EPS, ALU.mult, ALU.add))
                    link(v.tensor_scalar(t.bitcast(I32), m.bitcast(I32), 1, None, ALU.logical_shift_right))
                    link(v.tensor_scalar(y.bitcast(I32), t.bitcast(I32), -1.0, RSQRT_MAGIC, ALU.mult, ALU.add))
                    for _ in range(3):
                        link(v.scalar_tensor_tensor(t, y, m, y, ALU.mult, ALU.mult))
                        link(v.tensor_scalar(t, t, -0.5, 1.5, ALU.mult, ALU.add))
                        link(v.tensor_tensor(y, y, t, ALU.mult))
                    return y

                def split_h(ph, tt):
                    for hb in range(2):
                        dve.wait_ge(s_hhi, b * 16 + 8 * ph + 2 * tt + hb + 1)
                        a = slice(4 * hb, 4 * hb + 4), slice(tt * P, (tt + 1) * P)
                        v.tensor_tensor(h_lo[:, a[0], a[1]], banks[2 * (tt % 2) + hb].rearrange("p (k t) -> p k t", k=4),
                                        h_hi[:, a[0], a[1]].bitcast(F32), ALU.subtract).then_inc(s_hlo, 1)

                def norm(ph, src):
                    for tt in range(TT):
                        dve.wait_ge(s_sq, b * 24 + 8 * ph + (2 * tt + 2 if ph == 0 else 5 + tt))
                        y = rsqrt(ph, tt)
                        if tt >= 2:
                            dve.wait_ge(s_xt, b * 16 + 8 * ph + 2 * (tt - 2) + 2)
                        v.scalar_tensor_tensor(xs[tt % 2], src[:, tt, :], y, gains[ph][:, :],
                                               ALU.mult, ALU.mult).then_inc(s_xs, 1)
                        if tt:
                            split_h(ph, tt - 1)
                    split_h(ph, TT - 1)

                def split_y(k, full, signal):
                    link(v.tensor_copy(y_hi[:, k, :], full))
                    v.tensor_tensor(y_lo[:, k, :], full, y_hi[:, k, :].bitcast(F32), ALU.subtract).then_inc(signal, 1)

                norm(0, xin)
                for c in range(4):
                    q = c % 2
                    u, y, bk = conv_u[q], conv_y[q], 4 * q
                    step(v.tensor_copy(u[:, 0:2], conv_hist[:, c, :]))
                    dve.wait_ge(s_conv_c, b * 4 + c + 1)
                    wait_unit(dve, b, U_CONV + 4 * c + 1)
                    link(v.tensor_tensor(u[:, 2:2 + TB], conv_c[q], banks[bk + 1], ALU.mult))
                    step(v.tensor_copy(conv_hist[:, c, :], u[:, TB:TB + 2]))
                    link(v.tensor_scalar(y, u[:, 0:TB], conv_w[:, 0, c:c + 1], None, ALU.mult))
                    for k in (1, 2):
                        link(v.scalar_tensor_tensor(y, u[:, k:k + TB], conv_w[:, k, c:c + 1], y, ALU.mult, ALU.add))
                    wait_unit(dve, b, U_CONV + 4 * c + 2)
                    step(v.tensor_tensor(y, y, banks[bk + 2], ALU.mult))
                    dve.wait_ge(s_conv_t, b * 4 + c + 1)
                    link(v.scalar_tensor_tensor(conv_g[q], conv_t[q], 1.0, banks[bk + 3], ALU.add, ALU.mult))
                    link(v.scalar_tensor_tensor(y, y, 0.5, conv_g[q], ALU.mult, ALU.mult))
                    split_y(c, y, s_ye)

                def pool_pre(g):
                    q, w = g % 2, 2 << g
                    u, bufs = pool_u[q], (pool_s[q], pool_d[q])
                    step(v.tensor_copy(u[:, 0:16], pool_hist[:, g, :]))
                    dve.wait_ge(s_pool_u, b * 4 + g + 1)
                    sync()
                    step(v.tensor_copy(pool_hist[:, g, :], u[:, TB:TB + 16]))
                    src, off = u, 1
                    for level in range(g + 1):
                        dst = bufs[level % 2]
                        lo = 2 * off - 1
                        link(v.tensor_tensor(dst[:, lo:PW], src[:, lo:PW], src[:, lo - off:PW - off], ALU.add))
                        src, off = dst, 2 * off
                    link(v.tensor_tensor(src[:, 16:32], src[:, 16:32], corr[:, g, :], ALU.mult))
                    v.scalar_tensor_tensor(pool_diff[g][:, 16:PW], src[:, 16:PW], 1.0 / w, u[:, 16:PW],
                                           ALU.mult, ALU.subtract).then_inc(s_pool_diff, 1)
                    dve.wait_ge(s_pool_t, b * 4 + g + 1)
                    v.scalar_tensor_tensor(pool_g[q][:, 0:TB], pool_t[q][:, 0:TB], 1.0, banks[2 * q + 1],
                                           ALU.add, ALU.mult).then_inc(s_pool_gate, 1)

                def pool_end(g):
                    q = g % 2
                    dve.wait_ge(s_pm, b * 4 + g + 1)
                    dve.wait_ge(s_pool_gate, b * 4 + g + 1)
                    y = pool_t[q][:, 0:TB]
                    link(v.scalar_tensor_tensor(y, banks[4 + g], pool_sc[:, g:g + 1], pool_g[q][:, 0:TB],
                                                ALU.mult, ALU.mult))
                    split_y(4 + g, y, s_ye)

                pool_pre(0)
                for g in range(1, GROUPS):
                    pool_pre(g)
                    pool_end(g - 1)
                pool_end(GROUPS - 1)
                for n in range(2):
                    wait_unit(dve, b, U_EOUT + 4 * n + 3)
                    for tt in range(TT):
                        if n == 0:
                            dve.wait_ge(s_store[tt], b * 16 + 1)
                        c = slice(n * 512, n * 512 + 512)
                        v.tensor_tensor(res[:, tt, c], banks[4 * n + tt], xin[:, tt, c], ALU.add).then_inc(s_res, 1)
                norm(1, res)
                dve.wait_ge(s_grow, b + 1)
                step(v.tensor_scalar(row_u[:, :], banks[2][0:MH, :], ib[:, :], None, ALU.add))
                dve.wait_ge(s_row_abs, b + 1)
                step(v.tensor_scalar(row_m[:, :], banks[3][0:MH, :], fb[:, :], 0.0, ALU.add, ALU.min))
                dve.wait_ge(s_row_ln, b + 1)
                sync()
                link(v.tensor_tensor(row_m[:, :], row_m[:, :], row_t[:, :], ALU.subtract))
                step(v.tensor_tensor_scan(row_c[:, :], chunk_mask[:, :], row_m[:, :], 0.0, ALU.mult, ALU.add))
                link(v.memset(row_t[:, :], 0.0))
                step(v.tensor_tensor(row_u[:, :], row_u[:, :], row_c[:, :], ALU.subtract))
                step(v.tensor_copy(row_t[:, 0:1], carry_b[:, :]))
                step(v.tensor_tensor(m_prev[:, 0:1], carry_m[:, :], carry_b[:, :], ALU.add))
                link(v.tensor_copy(row_t[:, P:TB:P], row_c[:, P - 1:TB - 1:P]))
                link(v.tensor_tensor_scan(row_m[:, :], row_t[:, :], row_u[:, :], carry_m[:, :], ALU.add, ALU.max))
                step(v.tensor_tensor(m_prev[:, 1:TT], row_m[:, P - 1:TB - 1:P], row_c[:, P - 1:TB - 1:P], ALU.add))
                step(v.tensor_copy(carry_m[:, :], row_m[:, TB - 1:TB]))
                step(v.tensor_copy(carry_b[:, :], row_c[:, TB - 1:TB]))
                step(v.tensor_scalar(gate_rows[:, 3, :], row_m[:, :], -1.0, None, ALU.mult))
                link(v.scalar_tensor_tensor(gate_rows[:, 1, :], row_c[:, :], -1.0, row_m[:, :],
                                            ALU.mult, ALU.subtract))
                by_chunk = lambda r: r.rearrange("h (c t) -> h c t", c=TT)
                v.tensor_tensor(by_chunk(gate_rows[:, 2, :]), by_chunk(row_u[:, :]),
                                row_m[:, P - 1:TB:P].unsqueeze(2).broadcast_to([MH, TT, P]), ALU.subtract)
                v.tensor_tensor(by_chunk(gate_rows[:, 0, :]), by_chunk(gate_rows[:, 3, :]),
                                m_prev[:, :].unsqueeze(2).broadcast_to([MH, TT, P]), ALU.add).then_inc(s_rows_end, 1)

                def mem_pre(c):
                    q, a = c % 2, slice(c * P, (c + 1) * P)
                    dve.wait_ge(s_bc[q], b * 128 + 64 * (c // 2) + 64)
                    step(v.tensor_tensor(row_bc[q], row_bc[q], causal[:, :].unsqueeze(1).broadcast_to([P, MH, P]), ALU.add))
                    dve.wait_ge(s_ma, b * 4 + c + 1)
                    v.tensor_copy(cols[:, q, :], banks[5][:, 256:264]).then_inc(s_mem_masked, 1)
                    if c:
                        dve.wait_ge(s_mb, b * 4 + c)
                    for g in range(2):
                        r = slice(64 * g, 64 * g + 64)
                        step(v.tensor_tensor(q_inter[r, g:MH:2, :], q_mem[r, :, a], inter_bc[q][r], ALU.mult))
                    dve.wait_ge(s_mem_masked, b * 4 + c + 1)
                    step(v.tensor_tensor(k_wr, banks[5][:, 0:256].rearrange("p (h d) -> p h d", h=MH),
                                         cols[:, q, MH:2 * MH].unsqueeze(2).broadcast_to([P, MH, MD]), ALU.mult))
                    dve.wait_ge(s_mem_exp, b * 4 + c + 1)
                    v.tensor_tensor(decay_w, banks[4].rearrange("p (h t) -> p h t", h=MH), decay_w,
                                    ALU.mult).then_inc(s_mem_scored, 1)

                def mem_post(c):
                    q, a = c % 2, slice(c * P, (c + 1) * P)
                    dve.wait_ge(s_mb, b * 4 + c + 1)
                    for i in range(2):
                        last = v.scalar_tensor_tensor(state[:, i, :], state[:, i, :], inter_bc[q][:, i, P - 1:P],
                                                      banks[3][:, 256 * i:256 * i + 256], ALU.mult, ALU.add)
                    last.then_inc(s_mem_state, 1)
                    dve.wait_ge(s_mem_abs, b * 4 + c + 1)
                    link(v.tensor_tensor(recip, recip, emt_bc[q], ALU.max))
                    link(v.reciprocal(recip, recip))
                    v.tensor_tensor(mixed[:, 4:8, a], banks[6].rearrange("p (h t) -> p h t", h=MH), recip,
                                    ALU.mult).then_inc(s_mem_end, 1)

                for c in range(TT):
                    mem_pre(c)
                    mem_post(c)

                def att_add(p):
                    sbk, g, q = p // 2, p % 2, p % 2
                    dve.wait_ge(s_aa, b * 8 + p + 1)
                    if p >= 2:
                        dve.wait_ge(s_ab, b * 8 + p - 1)
                    sc, src = scores[:, 4 * q:4 * q + 4, :], pair_b[:, :, :].rearrange("p b (j k) -> p (b j) k", j=2)
                    bi = bias[:, 4 * g:4 * g + 4, :]
                    if sbk == 0:
                        v.scalar_tensor_tensor(sc[:, :, 0:P], src[:, :, 0:P], first[:, :], bi[:, :, 0:P], ALU.add, ALU.add)
                        v.tensor_tensor(sc[:, :, P:2 * P], src[:, :, P:2 * P], bi[:, :, P:2 * P],
                                        ALU.add).then_inc(s_att_added, 1)
                    else:
                        v.tensor_tensor(sc, src, bi, ALU.add).then_inc(s_att_added, 1)
                    dve.wait_ge(s_att_added, b * 8 + p + 1)
                    link(v.tensor_reduce(sm[:, q, 0:4], sc, AX.X, ALU.max))
                    link(v.scalar_tensor_tensor(sm[:, q, 4:8], sm[:, q, 0:4], -1.0, neg_sink[:, 4 * g:4 * g + 4],
                                                ALU.mult, ALU.min))
                    v.tensor_tensor(sm[:, q, 16:20], sm[:, q, 4:8], neg_sink[:, 4 * g:4 * g + 4],
                                    ALU.subtract).then_inc(s_att_max, 1)

                def att_norm(p):
                    q = p % 2
                    dve.wait_ge(s_att_exp, b * 8 + p + 1)
                    link(v.tensor_tensor(sm[:, q, 20:24], sm[:, q, 8:12], sm[:, q, 12:16], ALU.add))
                    link(v.reciprocal(sm[:, q, 20:24], sm[:, q, 20:24]))
                    for j in range(4):
                        last = v.tensor_scalar(scores[:, 4 * q + j, :], scores[:, 4 * q + j, :],
                                               sm[:, q, 20 + j:21 + j], None, ALU.mult)
                    last.then_inc(s_att_normed, 1)

                for s in range(12):
                    if s < PIECES:
                        att_add(s)
                    if 1 <= s < PIECES + 1:
                        att_norm(s - 1)
                    if 2 <= s < PIECES + 2:
                        p = s - 2
                        dve.wait_ge(s_ab, b * 8 + p + 1)
                        if p >= 2:
                            dve.wait_ge(s_ac, b * 8 + p - 1)
                        v.tensor_copy(probs_t[:, p % 2, 1, :], pair_c[:, 1, :]).then_inc(s_att_pv, 1)
                    if s < 8 and s % 2 == 1:
                        j = s // 2
                        dve.wait_ge(s_gate_t, b * 12 + s + 1)
                        step(v.scalar_tensor_tensor(gate_a, gate_tanh[0], 1.0, mixed[:, 4 + j, :], ALU.add, ALU.mult))
                        v.scalar_tensor_tensor(gate_b, gate_tanh[1], 1.0, banks[1], ALU.add, ALU.mult).then_inc(s_gated, 1)
                        dve.wait_ge(s_gated, b * 8 + j + 1)
                        link(v.scalar_tensor_tensor(gate_a, gate_a, 0.25, gate_b, ALU.mult, ALU.mult))
                        split_y(4 + j, gate_a, s_yo)
                    if s >= 8:
                        dve.wait_ge(s_gate_t, b * 12 + s + 1)
                        v.scalar_tensor_tensor(att_gate[:, s - 8, :], gate_tanh[s % 2], 1.0, banks[s % 2],
                                               ALU.add, ALU.mult).then_inc(s_gated, 1)
                dve.wait_ge(s_gated, b * 8 + 8)
                dve.wait_ge(s_att_out, b * 4 + 4)
                for j in range(4):
                    g = att_gate[:, j, :]
                    link(v.scalar_tensor_tensor(g, mixed[:, j, :], 0.5, g, ALU.mult, ALU.mult))
                    split_y(j, g, s_yo)
                for n in range(2):
                    wait_unit(dve, b, U_OOUT + 4 * n + 3)
                    for tt in range(TT):
                        c = slice(n * 512, n * 512 + 512)
                        v.tensor_tensor(res[:, tt, c], banks[4 * n + tt], res[:, tt, c], ALU.add).then_inc(s_fin, 1)
                for tt in range(TT):
                    dve.wait_ge(s_sq, b * 24 + 16 + 5 + tt)
                    y = rsqrt(2, tt)
                    v.scalar_tensor_tensor(res[:, tt, :], res[:, tt, :], y, gains[2][:, :],
                                           ALU.mult, ALU.mult).then_inc(s_norm, 1)
                step(v.memset(first[:, :], 0.0))
                step(v.memset(corr[:, :, :], 1.0))
                sync()
                assert count[0] == DVE_STEPS, count[0]


_INS = ['x', 'even_norm', 'even_w_in', 'even_conv_w', 'even_pool_w', 'even_pool_scale', 'even_w_out',
        'odd_norm', 'odd_w_in', 'odd_i_bias', 'odd_f_bias', 'odd_sinks', 'odd_w_out', 'final_norm']


def kernel(**inputs):
    import numpy as np
    import concourse.bacc as bacc
    from concourse.bass_utils import run_bass_kernel_spmd

    nc = bacc.Bacc("TRN2", target_bir_lowering=False, num_devices=1)
    arrays, args = {}, []
    for name in _INS:
        a = np.ascontiguousarray(inputs[name])
        arrays[f"in_{name}"] = a
        args.append(nc.dram_tensor(f"in_{name}", a.shape, mybir.dt.from_np(a.dtype), kind="ExternalInput").ap())
    args.append(nc.dram_tensor("result", (1, S, D), F32, kind="ExternalOutput").ap())
    trunk(nc, *args)
    r = run_bass_kernel_spmd(nc, [arrays], core_ids=[0])
    return r.results[0]["result"]
```

```python
from contextlib import ExitStack

import concourse.bass as bass
from concourse import mybir

F32 = mybir.dt.float32
F32R = mybir.dt.float32r
I32 = mybir.dt.int32
ALU = mybir.AluOpType
ACT = mybir.ActivationFunctionType
AX = mybir.AxisListType

P = 128
D = 1024
S = 2048
TB = 512
NB = S // TB
TT = TB // P
KT = D // P
HALF = D // 2
CONV = 512
GROUPS = 4
HEADS, KVH, HD = 8, 2, 64
MH, MD, ME = 4, 64, 128
EPS = 1e-6
MASKED = -1e30
QSCALE = 0.125
RSQRT_MAGIC = float(0x5F3759DF)

E_XA, E_BG, E_CG, E_GA, E_U, E_GB = (CONV * i for i in range(6))
O_CQ, O_CK, O_CV, O_GC, O_DQ, O_DK, O_DV, O_DI, O_DO = 0, 512, 640, 768, 1280, 1536, 1792, 2304, 2312
O_GD = O_DO + 512

U_CONV, U_POOL, U_EOUT = 0, 16, 24
U_DV, U_DK, U_DQ, U_CK, U_CV, U_CQ, U_DOGD, U_GC, U_OOUT = 32, 36, 38, 40, 41, 42, 46, 54, 58
UNITS = 66
STAGES, SLOTS = 3, 2
OOUT_ORDER = (2, 3, 0, 1)
PIECES = 2 * TT

POOL_SETUP = 52
CONSTS = 9
IDENT_STEPS = 2
DVE_STEPS = 187


def trunk(nc, x, even_norm, even_w_in, even_conv_w, even_pool_w, even_pool_scale, even_w_out,
          odd_norm, odd_w_in, odd_i_bias, odd_f_bias, odd_sinks, odd_w_out, final_norm, out):
    ew, ow = even_w_in[0], odd_w_in[0]
    ewo, owo = even_w_out[0], odd_w_out[0]
    rows_dram = nc.dram_tensor("gate_rows", [MH, 2, TB], F32, kind="Internal").ap()

    def chan_unit(w, col):
        return [(slice(0, P), w[:, col:col + P].rearrange("(k p) c -> p k c", p=P), None)]

    def head_pair_unit(w, col, j):
        return [(slice(0, P), w[:, col + 256 * g + 64 * j:col + 256 * g + 64 * j + 64]
                 .rearrange("(k p) c -> p k c", p=P), g) for g in range(KVH)]

    def row_unit(w, row, col):
        return [(slice(0, P), w[row:row + 2 * P, col:col + 512].rearrange("(k p) c -> p k c", p=P), "rows")]

    units = []
    for c in range(4):
        units += [chan_unit(ew, o + P * c) for o in (E_CG, E_XA, E_BG, E_GA)]
    for g in range(GROUPS):
        units += [chan_unit(ew, o + P * g) for o in (E_U, E_GB)]
    units += [row_unit(ewo, 256 * kp, 512 * n) for n in range(2) for kp in range(4)]
    units += [row_unit(ow, 256 * kp, O_DV) for kp in range(4)]
    units += [chan_unit(ow, O_DK + P * i) for i in range(2)]
    units += [chan_unit(ow, O_DQ + P * i) for i in range(2)]
    units += [chan_unit(ow, O_CK), chan_unit(ow, O_CV)]
    units += [head_pair_unit(ow, O_CQ, j) for j in range(4)]
    for j in range(4):
        units += [chan_unit(ow, O_DO + P * j), chan_unit(ow, O_GD + P * j)]
    units += [chan_unit(ow, O_GC + P * j) for j in range(4)]
    units += [row_unit(owo, 256 * kp, 512 * n) for n in range(2) for kp in OOUT_ORDER]
    assert len(units) == UNITS and UNITS % STAGES == 0 and UNITS % SLOTS == 0
    stage_total = [16 * sum(len(units[i]) for i in range(s, UNITS, STAGES)) for s in range(STAGES)]
    stage_upto = [16 * sum(len(units[j]) for j in range(i % STAGES, i + 1, STAGES)) for i in range(UNITS)]

    ctx = ExitStack()
    with ctx:
        def sb(name, shape, dt=F32):
            return ctx.enter_context(nc.sbuf_tensor(name, shape, dt))

        def sem(name):
            return ctx.enter_context(nc.semaphore(name))

        stage = [sb(f"stage{i}", [P, KT * P]) for i in range(STAGES)]
        w_hi = [sb(f"w_hi{i}", [P, KT * P], F32R) for i in range(SLOTS)]
        w_lo = [sb(f"w_lo{i}", [P, KT * P], F32R) for i in range(SLOTS)]
        h_hi = sb("h_hi", [P, KT, TB], F32R)
        h_lo = sb("h_lo", [P, KT, TB], F32R)
        y_hi = sb("y_hi", [P, KT, TB], F32R)
        y_lo = sb("y_lo", [P, KT, TB], F32R)
        xin = sb("xin", [P, TT, D])
        mixed = xin[:, :, :].rearrange("p t d -> p (t d)").rearrange("p (k t) -> p k t", k=KT)
        gate_rows = mixed[0:MH, 0:4, :]
        res = sb("res", [P, TT, D])
        gains = [sb(f"gain{i}", [P, D]) for i in range(3)]
        proj = sb("proj", [P, 12 * TB + MH * TT])
        q_att = proj[:, 0:4 * TB].rearrange("p (j t) -> p j t", j=4)
        q_mem = proj[:, 4 * TB:6 * TB].rearrange("p (j t) -> p j t", j=2)
        k_mem = proj[:, 6 * TB:8 * TB].rearrange("p (j t) -> p j t", j=2)
        v_mem = proj[:, 8 * TB:].rearrange("p (c h e) -> p c h e", c=TT, h=MH)
        PW = TB + 16
        distance, window = proj[:, 0:2 * P], proj[:, 2 * P:4 * P]
        conv_u = [proj[:, 5 * PW * i:5 * PW * i + 2 + TB] for i in range(2)]
        conv_y = [proj[:, 5 * PW * i + PW:5 * PW * i + PW + TB] for i in range(2)]
        conv_c = [proj[:, 5 * PW * i + 2 * PW:5 * PW * i + 2 * PW + TB] for i in range(2)]
        conv_t = [proj[:, 5 * PW * i + 3 * PW:5 * PW * i + 3 * PW + TB] for i in range(2)]
        conv_g = [proj[:, 5 * PW * i + 4 * PW:5 * PW * i + 4 * PW + TB] for i in range(2)]
        pool_u = [proj[:, 5 * PW * i:5 * PW * i + PW] for i in range(2)]
        pool_t = [proj[:, 5 * PW * i + PW:5 * PW * i + 2 * PW] for i in range(2)]
        pool_g = [proj[:, 5 * PW * i + 2 * PW:5 * PW * i + 3 * PW] for i in range(2)]
        pool_s = [proj[:, 5 * PW * i + 3 * PW:5 * PW * i + 4 * PW] for i in range(2)]
        pool_d = [proj[:, 5 * PW * i + 4 * PW:5 * PW * i + 5 * PW] for i in range(2)]
        pool_diff = [(pool_s, pool_d)[(g + 1) % 2][g % 2] for g in range(GROUPS)]
        work = sb("work", [P, 8 * TB])
        xs = [work[:, D * i:D * i + D] for i in range(2)]
        scores = work[:, 0:4 * TB].rearrange("p (i k) -> p i k", i=8)
        probs_t = work[:, 4 * TB:8 * TB].rearrange("p (i b n) -> p i b n", i=2, b=2)
        row_bc = [work[:, 768 * i:768 * i + 512].rearrange("p (h t) -> p h t", h=MH) for i in range(2)]
        inter_bc = [work[:, 768 * i + 512:768 * i + 768].rearrange("p (h t) -> p h t", h=2) for i in range(2)]
        decay_w = work[:, 1536:2048].rearrange("p (h t) -> p h t", h=MH)
        k_wr = work[:, 2048:2304].rearrange("p (h t) -> p h t", h=MH)
        mem_tok = [work[:, 2304 + 512 * i:2816 + 512 * i].rearrange("p (h e) -> p h e", h=MH) for i in range(2)]
        q_plain = sb("q_plain", [P, MH, P])
        q_inter = sb("q_inter", [P, MH, P])
        k_att = sb("k_att", [P, P + TB])
        v_att = sb("v_att", [P, TT + 1, P])
        state = sb("state", [P, 2, ME + 1])
        bias = sb("bias", [P, HEADS, 2 * P])
        causal = sb("causal", [P, P])
        ident = sb("ident", [P, P])
        ones = sb("ones", [P, TT, MH, 1])
        conv_hist = sb("conv_hist", [P, 4, 2])
        pool_hist = sb("pool_hist", [P, GROUPS, 16])
        pool_w = sb("pool_w", [P, GROUPS, P])
        conv_w = sb("conv_w", [P, 3, 4])
        pool_sc = sb("pool_sc", [P, GROUPS])
        corr = sb("corr", [P, GROUPS, 16])
        first = sb("first", [P, 1])
        neg_sink = sb("neg_sink", [P, HEADS])
        wg_raw = sb("wg_raw", [P, KT, 2 * MH])
        wg_hi = sb("wg_hi", [P, KT, 64 + MH], F32R)
        wg_lo = sb("wg_lo", [P, KT, 64 + MH], F32R)
        gate_bias = sb("gate_bias", [64 + MH, 1])
        ib, fb = gate_bias[0:MH, :], gate_bias[64:64 + MH, :]
        chunk_mask = sb("chunk_mask", [MH, TB])
        row_u = work[0:MH, 3328:3840]
        row_t = mixed[0:MH, 4, :]
        row_c = mixed[0:MH, 5, :]
        row_m = mixed[0:MH, 6, :]
        m_prev = sb("m_prev", [MH, TT])
        carry_m = sb("carry_m", [MH, 1])
        carry_b = sb("carry_b", [MH, 1])
        cols = sb("cols", [P, 2, 3 * MH])
        den = sb("den", [P, 2, MH])
        sums = sb("sums", [P, 3, TT, 2])
        rs = sb("rs", [P, TT, 5])
        root = sb("root", [P, 3, TT])
        inv_sum = sb("inv_sum", [P, 4, 4])
        sm = sb("sm", [P, 2, 20])
        junk = sb("junk", [P, HALF])
        eps = sb("eps", [P, 1])
        power = sb("power", [P, 1])
        cv_chan = junk[:, :]
        att_tok = cv_chan
        gate_tanh = [proj[:, (4 + i) * TB:(5 + i) * TB] for i in range(2)]
        gate_a, gate_b = proj[:, 6 * TB:7 * TB], proj[:, 7 * TB:8 * TB]
        att_gate = proj[:, 8 * TB:12 * TB].rearrange("p (j t) -> p j t", j=4)

        bank = [ctx.enter_context(nc.psum_tensor(f"bank{i}", [P, 512], F32)) for i in range(2)]
        pair_a = ctx.enter_context(nc.psum_tensor("pair_a", [P, 2, 512], F32))
        pair_b = ctx.enter_context(nc.psum_tensor("pair_b", [P, 2, 512], F32))
        pair_c = ctx.enter_context(nc.psum_tensor("pair_c", [P, 2, 512], F32))
        banks = [bank[0][:, :], bank[1][:, :], pair_a[:, 0, :], pair_a[:, 1, :],
                 pair_b[:, 0, :], pair_b[:, 1, :], pair_c[:, 0, :], pair_c[:, 1, :]]

        s_staged = [sem(f"staged{i}") for i in range(STAGES)]
        s_split = sem("split")
        s_slot = sem("slot_free")
        s_unit = sem("unit_done")
        s_x = [sem(f"x_in{i}") for i in range(TT)]
        s_const = sem("consts")
        s_gain = sem("gain0")
        s_pool = sem("pool_setup")
        s_vset = sem("vec_setup")
        s_sq = sem("squares")
        s_xs = sem("scaled")
        s_xt = sem("transposed")
        s_hhi = sem("h_hi_ready")
        s_hlo = sem("h_lo_ready")
        s_dve = sem("dve_step")
        s_whi = sem("whi")
        s_conv_c = sem("conv_c")
        s_conv_t = sem("conv_t")
        s_pool_u = sem("pool_u")
        s_pool_t = sem("pool_t")
        s_pool_diff = sem("pool_diff")
        s_pool_gate = sem("pool_gate")
        s_row_abs = sem("row_abs")
        s_row_exp = sem("row_exp")
        s_row_ln = sem("row_ln")
        s_rows_end = sem("rows_end")
        s_rows_exp = sem("rows_exp")
        s_k_mem = sem("k_mem")
        s_v_mem = sem("v_mem")
        s_q_mem = sem("q_mem")
        s_k_att = sem("k_att")
        s_hist = sem("hist")
        s_q_plain = sem("q_plain")
        s_cv_chan = sem("cv_chan")
        s_q_att = sem("q_att")
        s_v_att = sem("v_att")
        s_mem_masked = sem("mem_masked")
        s_mem_exp = sem("mem_exp")
        s_mem_scored = sem("mem_scored")
        s_mem_state = sem("mem_state")
        s_mem_normed = sem("mem_normed")
        s_mtr = sem("mem_transposed")
        s_mem_out = sem("mem_out")
        s_att_tr = sem("att_out_transposed")
        s_v_ones = sem("v_ones")
        s_att_added = sem("att_added")
        s_att_max = sem("att_max")
        s_att_exp = sem("att_exp")
        s_att_normed = sem("att_normed")
        s_att_pa = sem("att_pa")
        s_att_pv = sem("att_pv")
        s_att_out = sem("att_out")
        s_gate_t = sem("gate_t")
        s_gated = sem("gated")
        s_ye = sem("y_even_ready")
        s_yo = sem("y_odd_ready")
        s_pm = sem("pool_product")
        s_res = sem("res_ready")
        s_fin = sem("fin_ready")
        s_tile = sem("tile_done")
        s_rms = sem("rms_ready")
        s_rms_step = sem("rms_step")
        s_norm = sem("out_normed")
        s_store = [sem(f"stored{i}") for i in range(TT)]
        s_gmm = sem("gates_product")
        s_rowst = sem("rows_stored")
        s_bc = [sem(f"rows_bc{i}") for i in range(2)]
        s_cvt = sem("values_transposed")
        s_ma = sem("mem_scores")
        s_mb = sem("mem_products")
        s_aa = sem("att_scores")
        s_ab = sem("att_transposed")
        s_ac = sem("att_values")
        block = ctx.enter_context(nc.Block())

        def wait_unit(eng, b, u):
            eng.wait_ge(s_unit, b * UNITS + u + 1 + SLOTS)

        OUT0, OUT1, VALUES, OUT2, OUT3 = range(5)
        last_unit = (U_EOUT + 3, U_EOUT + 7, U_DV + 3, U_OOUT + 3, U_OOUT + 7)

        def wait_tile(eng, b, product, tt):
            if tt < TT - 1:
                eng.wait_ge(s_tile, b * 15 + 3 * product + tt + 1)
            else:
                wait_unit(eng, b, last_unit[product])

        @block.sync
        def _(sp):
            def load_unit(i):
                for parts, src, kind in units[i]:
                    dst = stage[i % STAGES]
                    if kind == "rows":
                        d = dst[parts, :].rearrange("p (k c) -> p k c", k=2)
                    else:
                        d = dst[parts, :].rearrange("p (k c) -> p k c", k=KT)
                        if kind is not None:
                            d = d[:, :, 64 * kind:64 * kind + 64]
                    sp.dma_start(d, src).then_inc(s_staged[i % STAGES], 16)

            x_rows = x[0]

            def load_x(row):
                for tt in range(TT):
                    sp.dma_start(xin[:, tt, :], x_rows[bass.ds(row + tt * P, P), :]).then_inc(s_x[tt], 16)

            load_x(0)
            with sp.Fori(0, NB) as b:
                for i in range(UNITS):
                    sp.wait_ge(s_split, b * UNITS + i + 1)
                    load_unit(i)
                    if i == U_OOUT + 4:
                        sp.wait_ge(s_yo, b * 8 + 8)
                        load_x(((b + 1) % NB) * TB)
                    if i in (U_CK, U_CK + 3, U_CK + 5):
                        for c in {U_CK: (0, 1), U_CK + 3: (2,), U_CK + 5: (3,)}[i]:
                            if c == 0:
                                sp.wait_ge(s_rowst, b * 32 + 32)
                            if c >= 2:
                                sp.wait_ge(s_mem_state, b * 4 + c - 1)
                            r = rows_dram[:, :, c * P:(c + 1) * P]
                            sp.dma_start(row_bc[c % 2], r[:, 1, :].partition_broadcast(P)).then_inc(s_bc[c % 2], 16)
                            for g in range(2):
                                sp.dma_start(inter_bc[c % 2][64 * g:64 * g + 64],
                                             r[g:MH:2, 0, :].partition_broadcast(64)).then_inc(s_bc[c % 2], 16)

        @block.gpsimd
        def _(pool):
            g = nc.gpsimd
            n = [0]

            def step(ins):
                n[0] += 1
                ins.then_inc(s_pool, 1)

            def sync():
                pool.wait_ge(s_pool, n[0])

            def select(tensor, compare, fill, base, pattern, multiplier):
                sync()
                step(g.affine_select(out=tensor, in_=tensor, compare_op=compare, fill=fill, base=base,
                                     pattern=pattern, channel_multiplier=multiplier))

            g.sem_inc(s_split, STAGES)
            step(g.memset(ident[:, :], 0.0))
            select(ident[:, :], ALU.not_equal, 1.0, 0, [[-1, P]], 1)
            assert n[0] == IDENT_STEPS
            step(g.memset(eps[:, :], D * EPS))
            step(g.memset(power[:, :], -0.5))
            step(g.memset(causal[:, :], 0.0))
            select(causal[:, :], ALU.is_ge, MASKED, 0, [[1, P]], -1)
            step(g.iota(distance, pattern=[[-1, 2 * P]], base=P, channel_multiplier=1,
                        allow_small_or_imprecise_dtypes=True))
            step(g.memset(window, 0.0))
            select(window, ALU.is_ge, MASKED, P, [[-1, 2 * P]], 1)
            select(window, ALU.is_gt, MASKED, 0, [[1, 2 * P]], -1)
            for t in (wg_hi[:, :, :].bitcast(F32), wg_lo[:, :, :].bitcast(F32), q_plain[:, :, :], q_inter[:, :, :],
                      k_att[:, :], v_att[:, :, :], state[:, :, :], conv_hist[:, :, :], pool_hist[:, :, :],
                      carry_m[:, :], carry_b[:, :]):
                step(g.memset(t, 0.0))
            step(g.memset(ones[:, :, :, :], 1.0))
            step(g.memset(first[:, :], MASKED))
            step(g.memset(chunk_mask[:, :], 1.0))
            step(g.memset(corr[:, :, :], 1.0))
            sync()
            step(g.memset(chunk_mask[:, 0:TB:P], 0.0))
            for k in range(GROUPS):
                w = 2 << k
                for t in range(w - 1):
                    step(g.memset(corr[:, k, t:t + 1], w / (t + 1.0)))
            assert n[0] == POOL_SETUP, n[0]
            sync()

            def rms(count, sq, ph, tt):
                o = rs[:, tt, 0:1]
                pool.wait_ge(s_sq, sq)
                g.tensor_tensor(o, sums[:, ph, tt, 0:1], sums[:, ph, tt, 1:2], ALU.add).then_inc(s_rms_step, 1)
                pool.wait_ge(s_rms_step, 2 * count + 1)
                g.tensor_tensor(o, o, eps[:, :], ALU.add).then_inc(s_rms_step, 1)
                pool.wait_ge(s_rms_step, 2 * count + 2)
                g.tensor_tensor(rs[:, tt, 4 - ph:5 - ph], o, power[:, :], ALU.pow).then_inc(s_rms, 1)

            for tt in range(TT):
                rms(tt, 2 * tt + 2, 0, tt)
            pool.wait_ge(s_const, 16 * CONSTS)
            for i in range(2):
                c, raw = slice(64 * i, 64 * i + MH), wg_raw[:, :, MH * i:MH * i + MH]
                step(g.tensor_scalar(wg_hi[:, :, c], raw, 1.0, 0.0, ALU.mult, ALU.add))
                sync()
                step(g.tensor_tensor(wg_lo[:, :, c], raw, wg_hi[:, :, c].bitcast(F32), ALU.subtract))
            with pool.Fori(0, NB) as b:
                for i in range(UNITS):
                    if i in (U_DV, U_DV + 1):
                        for tt in ((0, 1), (2, 3))[i - U_DV]:
                            rms(b * 8 + TT + tt, b * 24 + 8 + 5 + tt, 1, tt)
                    if i == U_OOUT + 5:
                        for tt in range(TT):
                            rms(b * 8 + 2 * TT + tt, b * 24 + 16 + 2 * tt + 2, 0, tt)
                    sg, sl = i % STAGES, i % SLOTS
                    pool.wait_ge(s_staged[sg], b * stage_total[sg] + stage_upto[i])
                    pool.wait_ge(s_unit, b * UNITS + i + 1)
                    g.sem_inc(s_slot)
                    g.tensor_scalar(w_hi[sl][:, :], stage[sg][:, :], 1.0, 0.0, ALU.mult, ALU.add).then_inc(s_whi, 1)
                    pool.wait_ge(s_whi, b * UNITS + i + 1)
                    g.tensor_tensor(w_lo[sl][:, :], stage[sg][:, :], w_hi[sl][:, :].bitcast(F32),
                                    ALU.subtract).then_inc(s_split, 1)

        @block.tensor
        def _(pe):
            t = nc.tensor

            def mm3(dst, l_hi, l_lo, r_hi, r_lo, start, stop):
                t.matmul(dst, l_hi, r_hi, start=start, stop=False)
                t.matmul(dst, l_hi, r_lo, start=False, stop=False)
                return t.matmul(dst, l_lo, r_hi, start=False, stop=stop)

            pe.wait_ge(s_pool, IDENT_STEPS)
            pe.sem_inc(s_unit, SLOTS)
            pe.sem_inc(s_fin, 1)

            def transposes(count, tt):
                pe.wait_ge(s_xs, count + 1)
                for hb in range(2):
                    for q in range(4):
                        k = 4 * hb + q
                        last = t.transpose(banks[2 * (tt % 2) + hb][:, q * P:(q + 1) * P],
                                           xs[tt % 2][:, k * P:(k + 1) * P], ident[:, :])
                    last.then_inc(s_xt, 1)

            for tt in range(TT):
                if tt >= 2:
                    pe.wait_ge(s_hlo, 2 * (tt - 2) + 2)
                transposes(tt, tt)
            pe.wait_ge(s_pool, POOL_SETUP + 4)
            pe.wait_ge(s_const, 16 * CONSTS)
            with pe.Fori(0, NB) as b:
                def chan(u, dst):
                    pe.wait_ge(s_split, b * UNITS + u + 1 + STAGES)
                    sl = u % SLOTS
                    for k in range(KT):
                        last = mm3(dst, w_hi[sl][:, k * P:(k + 1) * P], w_lo[sl][:, k * P:(k + 1) * P],
                                   h_hi[:, k, :], h_lo[:, k, :], k == 0, k == KT - 1)
                    last.then_inc(s_unit, 1)

                def token_part(u, kp, tt, src_hi, src_lo, base, start, stop):
                    sl, a = u % SLOTS, slice(tt * P, (tt + 1) * P)
                    for kk in range(2):
                        k, c = 2 * kp + kk, slice(512 * kk, 512 * kk + 512)
                        last = mm3(banks[base + tt], src_hi[:, k, a], src_lo[:, k, a],
                                   w_hi[sl][:, c], w_lo[sl][:, c], start and kk == 0, stop and kk == 1)
                    return last

                def token(u, kp, src_hi, src_lo, base, start, stop):
                    pe.wait_ge(s_split, b * UNITS + u + 1 + STAGES)
                    for tt in range(TT):
                        last = token_part(u, kp, tt, src_hi, src_lo, base, start, stop)
                        if stop and tt < TT - 1:
                            last.then_inc(s_tile, 1)
                    last.then_inc(s_unit, 1)

                pe.wait_ge(s_hlo, b * 16 + 8)
                for c in range(4):
                    for j in range(4):
                        if c >= 2 and j == 0:
                            pe.wait_ge(s_ye, b * 8 + c - 1)
                        if c == 1 and j == 0:
                            pe.wait_ge(s_fin, b * 8 + 1)
                        chan(U_CONV + 4 * c + j, banks[4 * (c % 2) + j])

                def pool_product(g):
                    pe.wait_ge(s_pool_diff, b * 4 + g + 1)
                    t.matmul(banks[4 + g], pool_w[:, g, :], pool_diff[g][:, 16:PW], start=True, stop=True
                             ).then_inc(s_pm, 1)

                for g in range(GROUPS):
                    if g == 0:
                        pe.wait_ge(s_ye, b * 8 + 3)
                    if g >= 2:
                        pe.wait_ge(s_pool_gate, b * 4 + g - 1)
                    for j in range(2):
                        chan(U_POOL + 2 * g + j, banks[2 * (g % 2) + j])
                    if g == 1:
                        pe.wait_ge(s_ye, b * 8 + 4)
                    if g >= 1:
                        pool_product(g - 1)
                def tile(tt):
                    return b * 8 + TT + tt

                pe.wait_ge(s_pool_gate, b * 4 + 4)
                for kp in range(4):
                    if kp == 1:
                        pool_product(3)
                    if kp == 2:
                        pe.wait_ge(s_ye, b * 8 + 8)
                    token(U_EOUT + kp, kp, y_hi, y_lo, 0, kp == 0, kp == 3)
                for kp in range(2):
                    token(U_EOUT + 4 + kp, kp, y_hi, y_lo, 4, kp == 0, False)
                pe.wait_ge(s_split, b * UNITS + U_EOUT + 7 + STAGES)
                for kp, tt in ((2, 0), (2, 1), (2, 2), (3, 0), (2, 3), (3, 1), (3, 2), (3, 3)):
                    if (kp, tt) == (3, 0):
                        pe.wait_ge(s_split, b * UNITS + U_EOUT + 8 + STAGES)
                    last = token_part(U_EOUT + 4 + kp, kp, tt, y_hi, y_lo, 4, False, kp == 3)
                    if tt == TT - 1:
                        last.then_inc(s_unit, 1)
                    elif kp == 3:
                        last.then_inc(s_tile, 1)
                    if (kp, tt) == (3, 2):
                        pe.wait_ge(s_res, b * 8 + 4)
                        transposes(tile(0), 0)
                transposes(tile(1), 1)
                pe.wait_ge(s_split, b * UNITS + U_DV + 1 + STAGES)
                for kp, tt in ((0, 0), (0, 1), (1, 0), (0, 2), (0, 3), (1, 1), (1, 2), (1, 3)):
                    if kp == 0:
                        pe.wait_ge(s_hlo, 2 * tile(tt) + 2)
                        pe.wait_ge(s_res, b * 8 + 5 + tt)
                    elif tt == 0:
                        pe.wait_ge(s_split, b * UNITS + U_DV + 2 + STAGES)
                    last = token_part(U_DV + kp, kp, tt, h_hi, h_lo, 4, kp == 0, False)
                    if tt == TT - 1:
                        last.then_inc(s_unit, 1)
                    if kp == 0 and tt < 2:
                        transposes(tile(tt + 2), tt + 2)
                token(U_DV + 2, 2, h_hi, h_lo, 4, False, False)
                token(U_DV + 3, 3, h_hi, h_lo, 4, False, True)
                for k in range(KT):
                    last = mm3(banks[2][0:64 + MH, :], wg_hi[:, k, :], wg_lo[:, k, :], h_hi[:, k, :], h_lo[:, k, :],
                               k == 0, k == KT - 1)
                last.then_inc(s_gmm, 1)
                chan(U_DK, banks[0])
                chan(U_DK + 1, banks[1])

                def mem_a(c):
                    pe.wait_ge(s_q_plain, b * 4 + c + 1)
                    a = slice(c * P, (c + 1) * P)
                    if c == 0:
                        pe.wait_ge(s_v_mem, b * 4 + 4)
                        pe.wait_ge(s_v_ones, b + 1)
                        pe.wait_ge(s_q_mem, b * 2 + 2)
                        pe.wait_ge(s_rows_exp, b + 1)
                        pe.wait_ge(s_rows_end, b + 1)
                    else:
                        pe.wait_ge(s_mem_scored, b * 4 + c)
                    for i in range(2):
                        t.transpose(banks[5][:, i * P:(i + 1) * P], k_mem[:, i, a], ident[:, :])
                    t.transpose(banks[5][:, 256:260], row_u[:, a], ident[0:MH, 0:MH])
                    t.transpose(banks[5][:, 260:264], gate_rows[:, 2, a], ident[0:MH, 0:MH])
                    t.transpose(banks[5][:, 264:268], gate_rows[:, 1, a], ident[0:MH, 0:MH])
                    for h in range(MH):
                        last = t.matmul(banks[4][:, h * P:(h + 1) * P], k_mem[:, h // 2, a],
                                        q_plain[:, h, :], start=True, stop=True)
                    last.then_inc(s_ma, 1)

                def mem_b(c):
                    pe.wait_ge(s_mem_scored, b * 4 + c + 1)
                    if c:
                        pe.wait_ge(s_mem_state, b * 4 + c)
                        pe.wait_ge(s_mem_normed, b * 4 + c)
                    for h in range(MH):
                        dst = pair_c[:, h // 2, 129 * (h % 2):129 * (h % 2) + 129]
                        t.matmul(dst, decay_w[:, h, :], v_mem[:, c, h, :], start=True, stop=False)
                        t.matmul(dst, q_inter[:, h, :], state[:, h // 2, :], start=False, stop=True)
                    for h in range(MH):
                        r = slice(64 * (h % 2), 64 * (h % 2) + 64)
                        last = t.matmul(banks[3][r, 129 * (h // 2):129 * (h // 2) + 129], k_wr[:, h, :],
                                        v_mem[:, c, h, :], start=True, stop=True)
                    last.then_inc(s_mb, 1)

                def mem_t(c):
                    pe.wait_ge(s_mem_normed, b * 4 + c + 1)
                    if c:
                        pe.wait_ge(s_mem_out, b * 4 + c)
                    else:
                        pe.wait_ge(s_v_att, b + 1)
                    for h in range(MH):
                        last = t.transpose(banks[2][:, h * P:(h + 1) * P], mem_tok[c % 2][:, h, :], ident[:, :])
                    last.then_inc(s_mtr, 1)

                pe.wait_ge(s_k_mem, b * 2 + 1)
                chan(U_DQ, banks[0])
                pe.wait_ge(s_k_mem, b * 2 + 2)
                chan(U_DQ + 1, banks[1])
                pe.wait_ge(s_q_mem, b * 2 + 1)
                chan(U_CK, banks[0])
                mem_a(0)
                pe.wait_ge(s_q_mem, b * 2 + 2)
                chan(U_CV, banks[1])
                mem_b(0)
                mem_a(1)
                pe.wait_ge(s_k_att, b + 1)
                chan(U_CQ, banks[0])
                pe.wait_ge(s_cv_chan, b + 1)
                for tt in range(TT):
                    last = t.transpose(banks[2][:, tt * P:(tt + 1) * P], cv_chan[:, tt * P:(tt + 1) * P], ident[:, :])
                last.then_inc(s_cvt, 1)
                mem_b(1)
                mem_a(2)
                chan(U_CQ + 1, banks[1])
                mem_t(0)
                mem_b(2)
                mem_a(3)
                pe.wait_ge(s_q_att, b * 4 + 1)
                chan(U_CQ + 2, banks[0])
                mem_t(1)
                mem_b(3)
                pe.wait_ge(s_q_att, b * 4 + 2)
                chan(U_CQ + 3, banks[1])
                mem_t(2)
                pe.wait_ge(s_q_att, b * 4 + 4)
                pe.wait_ge(s_v_att, b + 1)

                def att_a(p):
                    sbk, g = p // 2, p % 2
                    r = slice(64 * g, 64 * g + 64)
                    if p:
                        pe.wait_ge(s_att_added, b * 8 + p)
                    for j in range(4):
                        last = t.matmul(pair_b[:, j // 2, 256 * (j % 2):256 * (j % 2) + 256],
                                        q_att[r, j, sbk * P:(sbk + 1) * P], k_att[r, sbk * P:(sbk + 2) * P],
                                        start=True, stop=True)
                    last.then_inc(s_aa, 1)

                def att_b(p):
                    pe.wait_ge(s_att_exp, b * 8 + p + 1)
                    if p:
                        pe.wait_ge(s_att_pa, b * 8 + p)
                        pe.wait_ge(s_att_pv, b * 8 + p)
                    for kb in range(2):
                        for j in range(4):
                            last = t.transpose(pair_c[:, kb, j * P:(j + 1) * P],
                                               scores[:, 4 * (p % 2) + j, kb * P:(kb + 1) * P], ident[:, :])
                    last.then_inc(s_ab, 1)

                def att_c(p):
                    sbk, g = p // 2, p % 2
                    pe.wait_ge(s_att_pa, b * 8 + p + 1)
                    pe.wait_ge(s_att_pv, b * 8 + p + 1)
                    if p:
                        pe.wait_ge(s_att_normed, b * 8 + p)
                    else:
                        pe.wait_ge(s_mem_out, b * 4 + 4)
                    for j in range(4):
                        dst = banks[2][:, 256 * g + HD * j:256 * g + HD * (j + 1)]
                        for kb in range(2):
                            last = t.matmul(dst, probs_t[:, p % 2, kb, j * P:(j + 1) * P],
                                            v_att[:, sbk + kb, HD * g:HD * (g + 1)], start=kb == 0, stop=kb == 1)
                    last.then_inc(s_ac, 1)

                def att_t(sbk):
                    pe.wait_ge(s_att_normed, b * 8 + 2 * sbk + 2)
                    if sbk:
                        pe.wait_ge(s_att_out, b * 4 + sbk)
                    else:
                        pe.wait_ge(s_mem_state, b * 4 + 4)
                    for j in range(4):
                        last = t.transpose(banks[3][:, j * P:(j + 1) * P], att_tok[:, j * P:(j + 1) * P], ident[:, :])
                    last.then_inc(s_att_tr, 1)

                for s in range(12):
                    if s == 1:
                        mem_t(TT - 1)
                    if 5 <= s and s % 2 == 1:
                        att_t((s - 5) // 2)
                    if 2 <= s < PIECES + 2:
                        att_b(s - 2)
                    if 3 <= s < PIECES + 3:
                        att_c(s - 3)
                    if s < PIECES:
                        att_a(s)
                    if s in (2, 4, 6, 8):
                        pe.wait_ge(s_gate_t, b * 12 + s - 1)
                    elif s > 1:
                        pe.wait_ge(s_gated, b * 8 + (s - 1) // 2 if s < 10 else b * 8 + s - 5)
                    chan(U_DOGD + s, banks[s % 2])
                pe.wait_ge(s_yo, b * 8 + 4)
                pe.wait_ge(s_gated, b * 8 + 7)
                pe.wait_ge(s_att_out, b * 4 + 4)
                pe.wait_ge(s_split, b * UNITS + U_OOUT + 1 + STAGES)
                for tt in (0, 2, 3, 1):
                    if tt == 1:
                        pe.wait_ge(s_gated, b * 8 + 8)
                    last = token_part(U_OOUT, OOUT_ORDER[0], tt, y_hi, y_lo, 0, True, False)
                last.then_inc(s_unit, 1)
                for i in (1, 2, 3):
                    if i == 2:
                        pe.wait_ge(s_yo, b * 8 + 8)
                    token(U_OOUT + i, OOUT_ORDER[i], y_hi, y_lo, 0, False, i == 3)
                for i, kp in enumerate(OOUT_ORDER):
                    token(U_OOUT + 4 + i, kp, y_hi, y_lo, 4, i == 0, i == 3)
                    for tt in ((0, 1), (2,), (3,), ())[i]:
                        if tt < 2:
                            pe.wait_ge(s_fin, b * 8 + 4 + 1)
                        else:
                            pe.wait_ge(s_hlo, 2 * (b * 8 + 2 * TT + tt - 2) + 2)
                        transposes(b * 8 + 2 * TT + tt, tt)

        @block.scalar
        def _(act):
            a = nc.scalar
            act.dma_start(gains[0][:, :], even_norm[0].partition_broadcast(P)).then_inc(s_gain, 16)
            for dst, src in (
                    (gains[1][:, :], odd_norm[0].partition_broadcast(P)),
                    (gains[2][:, :], final_norm.partition_broadcast(P)),
                    (pool_w[:, :, :], even_pool_w[0].rearrange("g c d -> c g d")),
                    (conv_w[:, :, :], even_conv_w[0].rearrange("k (c p) -> p k c", p=P)),
                    (pool_sc[:, :], even_pool_scale[0].rearrange("(g p) -> p g", p=P)),
                    (neg_sink[:, :], odd_sinks[0].partition_broadcast(P)),
                    (wg_raw[:, :, :], ow[:, O_DI:O_DI + 2 * MH].rearrange("(k p) c -> p k c", p=P)),
                    (ib, odd_i_bias[0].rearrange("(h o) -> h o", o=1)),
                    (fb, odd_f_bias[0].rearrange("(h o) -> h o", o=1))):
                act.dma_start(dst, src, allow_slow_non_contiguous=True).then_inc(s_const, 16)
            out_rows = out[0]
            for tt in range(TT):
                act.sem_inc(s_store[tt], 1)

            def square(number, ph, src, tt, hf):
                if number is not None:
                    act.wait_ge(s_sq, number)
                a.activation(junk[:, :], src[:, tt, hf * HALF:(hf + 1) * HALF], ACT.Square,
                             accum_out=sums[:, ph, tt, hf:hf + 1]).then_inc(s_sq, 1)

            def evacuate(count, tt):
                for hb in range(2):
                    act.wait_ge(s_xt, 2 * count + hb + 1)
                    a.activation(h_hi[:, 4 * hb:4 * hb + 4, tt * P:(tt + 1) * P],
                                 banks[2 * (tt % 2) + hb].rearrange("p (k t) -> p k t", k=4),
                                 ACT.Copy).then_inc(s_hhi, 1)

            for tt in range(TT):
                act.wait_ge(s_x[tt], 16)
                for hf in range(2):
                    square(2 * tt + hf if tt + hf else None, 0, xin, tt, hf)
                if tt:
                    evacuate(tt - 1, tt - 1)
            evacuate(TT - 1, TT - 1)
            act.wait_ge(s_const, 16 * CONSTS)
            act.wait_ge(s_pool, POOL_SETUP)
            with act.Fori(0, NB) as b:
                sq = b * 24 + 8
                for c in range(4):
                    wait_unit(act, b, U_CONV + 4 * c)
                    if c >= 2:
                        act.wait_ge(s_ye, b * 8 + c - 1)
                    a.activation(conv_c[c % 2], banks[4 * (c % 2)], ACT.Copy).then_inc(s_conv_c, 1)
                    wait_unit(act, b, U_CONV + 4 * c + 3)
                    a.activation(conv_t[c % 2], banks[4 * (c % 2) + 3], ACT.Tanh, scale=0.5).then_inc(s_conv_t, 1)
                for g in range(GROUPS):
                    wait_unit(act, b, U_POOL + 2 * g)
                    act.wait_ge(s_ye, b * 8 + 3 + g)
                    a.activation(pool_u[g % 2][:, 16:PW], banks[2 * (g % 2)], ACT.Copy).then_inc(s_pool_u, 1)
                    wait_unit(act, b, U_POOL + 2 * g + 1)
                    a.activation(pool_t[g % 2][:, 0:TB], banks[2 * (g % 2) + 1], ACT.Tanh,
                                 scale=0.5).then_inc(s_pool_t, 1)
                for tt in range(TT):
                    act.wait_ge(s_res, b * 8 + tt + 1)
                    square(sq + tt, 1, res, tt, 0)
                for tt in range(TT):
                    act.wait_ge(s_res, b * 8 + 4 + tt + 1)
                    square(sq + 4 + tt, 1, res, tt, 1)
                    if tt == 1:
                        evacuate(b * 8 + TT, 0)
                for tt in range(1, TT):
                    evacuate(b * 8 + TT + tt, tt)
                a.activation(v_mem[:, :, :, ME:ME + 1], ones[:, :, :, :], ACT.Copy).then_inc(s_v_ones, 1)
                for tt in range(TT):
                    wait_tile(act, b, VALUES, tt)
                    a.activation(v_mem[:, tt, :, 0:ME], banks[4 + tt].rearrange("p (h e) -> p h e", h=MH),
                                 ACT.Copy).then_inc(s_v_mem, 1)
                act.wait_ge(s_gmm, b + 1)
                a.activation(row_t[:, :], banks[2][64:64 + MH, :], ACT.Abs, bias=fb).then_inc(s_row_abs, 1)
                act.wait_ge(s_row_abs, b + 1)
                a.activation(row_t[:, :], row_t[:, :], ACT.Exp, scale=-1.0).then_inc(s_row_exp, 1)
                act.wait_ge(s_row_exp, b + 1)
                a.activation(row_t[:, :], row_t[:, :], ACT.Ln, bias=1.0).then_inc(s_row_ln, 1)
                for i in range(2):
                    wait_unit(act, b, U_DK + i)
                    a.activation(k_mem[:, i, :], banks[i], ACT.Copy).then_inc(s_k_mem, 1)
                act.wait_ge(s_rows_end, b + 1)
                a.activation(gate_rows[:, 0:3, :], gate_rows[:, 0:3, :], ACT.Exp).then_inc(s_rows_exp, 1)
                act.wait_ge(s_rows_exp, b + 1)
                act.dma_start(rows_dram[:, 0, :], gate_rows[:, 0, :]).then_inc(s_rowst, 16)
                act.dma_start(rows_dram[:, 1, :], gate_rows[:, 3, :]).then_inc(s_rowst, 16)
                for i in range(2):
                    wait_unit(act, b, U_DQ + i)
                    a.activation(q_mem[:, i, :], banks[i], ACT.Copy, scale=QSCALE).then_inc(s_q_mem, 1)

                def mem_q(c):
                    if c:
                        act.wait_ge(s_ma, b * 4 + c)
                    else:
                        act.wait_ge(s_q_mem, b * 2 + 2)
                    for g in range(2):
                        last = a.activation(q_plain[64 * g:64 * g + 64, g:MH:2, :],
                                            q_mem[64 * g:64 * g + 64, :, c * P:(c + 1) * P], ACT.Copy)
                    last.then_inc(s_q_plain, 1)

                def mem_exp(c):
                    act.wait_ge(s_mem_masked, b * 4 + c + 1)
                    if c:
                        act.wait_ge(s_mb, b * 4 + c)
                    for h in range(MH):
                        last = a.activation(decay_w[:, h, :], row_bc[c % 2][:, h, :], ACT.Exp,
                                            bias=cols[:, c % 2, h:h + 1])
                    last.then_inc(s_mem_exp, 1)
                    if c < TT - 1:
                        mem_q(c + 1)

                def mem_out(c):
                    act.wait_ge(s_mtr, b * 4 + c + 1)
                    a.activation(mixed[:, 4:8, c * P:(c + 1) * P], banks[2].rearrange("p (h t) -> p h t", h=MH),
                                 ACT.Copy).then_inc(s_mem_out, 1)

                def att_query(j):
                    wait_unit(act, b, U_CQ + j)
                    a.activation(q_att[:, j, :], banks[j % 2], ACT.Copy, scale=QSCALE).then_inc(s_q_att, 1)

                a.activation(k_att[:, 0:P], k_att[:, TB:TB + P], ACT.Copy).then_inc(s_hist, 1)
                a.activation(v_att[:, 0, :], v_att[:, TT, :], ACT.Copy).then_inc(s_hist, 1)
                mem_q(0)
                wait_unit(act, b, U_CK)
                act.wait_ge(s_hist, b * 2 + 2)
                a.activation(k_att[:, P:P + TB], banks[0], ACT.Copy).then_inc(s_k_att, 1)
                mem_exp(0)
                wait_unit(act, b, U_CV)
                a.activation(cv_chan[:, :], banks[1], ACT.Copy).then_inc(s_cv_chan, 1)
                mem_exp(1)
                att_query(0)
                act.wait_ge(s_cvt, b + 1)
                a.activation(v_att[:, 1:TT + 1, :], banks[2].rearrange("p (t c) -> p t c", t=TT),
                             ACT.Copy).then_inc(s_v_att, 1)
                mem_exp(2)
                att_query(1)
                mem_out(0)
                mem_exp(3)
                att_query(2)
                mem_out(1)
                att_query(3)
                mem_out(2)

                def att_exp(p):
                    q = p % 2
                    act.wait_ge(s_att_max, b * 8 + p + 1)
                    for j in range(4):
                        a.activation(scores[:, 4 * q + j, :], scores[:, 4 * q + j, :], ACT.Exp,
                                     bias=sm[:, q, 4 + j:5 + j], accum_out=sm[:, q, 8 + j:9 + j])
                    a.activation(sm[:, q, 12:16], sm[:, q, 16:20], ACT.Exp).then_inc(s_att_exp, 1)

                for s in range(12):
                    if s == 1:
                        mem_out(3)
                    if s >= 5 and s % 2 == 1:
                        sbk = (s - 5) // 2
                        act.wait_ge(s_att_tr, b * 4 + sbk + 1)
                        a.activation(mixed[:, 0:4, sbk * P:(sbk + 1) * P],
                                     banks[3].rearrange("p (j t) -> p j t", j=4), ACT.Copy).then_inc(s_att_out, 1)
                    if 2 <= s < PIECES + 2:
                        p = s - 2
                        act.wait_ge(s_ab, b * 8 + p + 1)
                        if p >= 2:
                            act.wait_ge(s_ac, b * 8 + p - 1)
                        a.activation(probs_t[:, p % 2, 0, :], pair_c[:, 0, :], ACT.Copy).then_inc(s_att_pa, 1)
                    if s < PIECES:
                        att_exp(s)
                    wait_unit(act, b, U_DOGD + s)
                    if s >= 2:
                        act.wait_ge(s_gated, b * 8 + (s // 2 if s < 9 else s - 5))
                    a.activation(gate_tanh[s % 2], banks[s % 2], ACT.Tanh, scale=0.5).then_inc(s_gate_t, 1)

                for tt in range(TT):
                    act.wait_ge(s_x[tt], b * 16 + 32)
                    for hf in range(2):
                        square(sq + 8 + 2 * tt + hf, 0, xin, tt, hf)
                for tt in range(TT):
                    act.wait_ge(s_fin, b * 8 + tt + 1 + 1)
                    square(sq + 16 + tt, 2, res, tt, 0)
                for tt in range(TT):
                    evacuate(b * 8 + 2 * TT + tt, tt)
                for tt in range(TT):
                    act.wait_ge(s_fin, b * 8 + 4 + tt + 1 + 1)
                    square(sq + 20 + tt, 2, res, tt, 1)
                for tt in range(TT):
                    act.wait_ge(s_norm, b * 4 + tt + 1)
                    act.dma_start(out_rows[bass.ds(b * TB + tt * P, P), :], res[:, tt, :]).then_inc(s_store[tt], 16)
            for tt in range(TT):
                act.wait_ge(s_store[tt], 16 * NB + 1)

        @block.vector
        def _(dve):
            v = nc.vector
            dve.wait_ge(s_gain, 16)
            v.tensor_scalar(gains[0][:, :], gains[0][:, :], float(D) ** 0.5, None, ALU.mult).then_inc(s_vset, 1)
            dve.wait_ge(s_vset, 1)

            def scale(count, ph, src, tt):
                dve.wait_ge(s_rms, count + 1)
                if tt >= 2:
                    dve.wait_ge(s_xt, 2 * (count - 2) + 2)
                v.scalar_tensor_tensor(xs[tt % 2], src[:, tt, :], rs[:, tt, 4 - ph:5 - ph], gains[ph][:, :],
                                       ALU.mult, ALU.mult).then_inc(s_xs, 1)

            def split_h(count, tt):
                for hb in range(2):
                    dve.wait_ge(s_hhi, 2 * count + hb + 1)
                    ks, ts = slice(4 * hb, 4 * hb + 4), slice(tt * P, (tt + 1) * P)
                    v.tensor_tensor(h_lo[:, ks, ts], banks[2 * (tt % 2) + hb].rearrange("p (k t) -> p k t", k=4),
                                    h_hi[:, ks, ts].bitcast(F32), ALU.subtract).then_inc(s_hlo, 1)

            def norm(first_tile, ph, src):
                for tt in range(TT):
                    scale(first_tile + tt, ph, src, tt)
                    if tt:
                        split_h(first_tile + tt - 1, tt - 1)
                split_h(first_tile + TT - 1, TT - 1)

            norm(0, 0, xin)
            dve.wait_ge(s_const, 16 * CONSTS)
            dve.wait_ge(s_pool, POOL_SETUP)
            v.tensor_scalar(gains[1][:, :], gains[1][:, :], float(D) ** 0.5, None, ALU.mult).then_inc(s_vset, 1)
            v.tensor_scalar(pool_sc[:, :], pool_sc[:, :], 0.5, None, ALU.mult).then_inc(s_vset, 1)
            v.tensor_scalar(neg_sink[:, :], neg_sink[:, :], -1.0, None, ALU.mult).then_inc(s_vset, 1)
            for h in range(HEADS):
                v.scalar_tensor_tensor(bias[:, h, :], distance, -2.0 ** (-8.0 * (h + 1) / HEADS), window,
                                       ALU.mult, ALU.add).then_inc(s_vset, 1)
            dve.wait_ge(s_vset, 4 + HEADS)
            with dve.Fori(0, NB) as b:
                count = [0]

                def step(ins):
                    ins.then_inc(s_dve, 1)
                    count[0] += 1

                def sync():
                    dve.wait_ge(s_dve, b * DVE_STEPS + count[0])

                def link(ins):
                    step(ins)
                    sync()

                def rsqrt():
                    m, t, y = root[:, 0, :], root[:, 1, :], root[:, 2, :]
                    link(v.tensor_tensor(m, sums[:, 2, :, 0], sums[:, 2, :, 1], ALU.add))
                    link(v.tensor_scalar(m, m, 1.0 / D, EPS, ALU.mult, ALU.add))
                    link(v.tensor_scalar(t.bitcast(I32), m.bitcast(I32), 1, None, ALU.logical_shift_right))
                    link(v.tensor_scalar(y.bitcast(I32), t.bitcast(I32), -1.0, RSQRT_MAGIC, ALU.mult, ALU.add))
                    for _ in range(3):
                        link(v.tensor_tensor(t, y, y, ALU.mult))
                        link(v.tensor_tensor(t, t, m, ALU.mult))
                        link(v.tensor_scalar(t, t, -0.5, 1.5, ALU.mult, ALU.add))
                        link(v.tensor_tensor(y, y, t, ALU.mult))

                def split_y(k, full, signal):
                    link(v.tensor_copy(y_hi[:, k, :], full))
                    v.tensor_tensor(y_lo[:, k, :], full, y_hi[:, k, :].bitcast(F32), ALU.subtract).then_inc(signal, 1)

                for c in range(4):
                    q = c % 2
                    u, y, bk = conv_u[q], conv_y[q], 4 * q
                    step(v.tensor_copy(u[:, 0:2], conv_hist[:, c, :]))
                    dve.wait_ge(s_conv_c, b * 4 + c + 1)
                    wait_unit(dve, b, U_CONV + 4 * c + 1)
                    link(v.tensor_tensor(u[:, 2:2 + TB], conv_c[q], banks[bk + 1], ALU.mult))
                    step(v.tensor_copy(conv_hist[:, c, :], u[:, TB:TB + 2]))
                    link(v.tensor_scalar(y, u[:, 0:TB], conv_w[:, 0, c:c + 1], None, ALU.mult))
                    for k in (1, 2):
                        link(v.scalar_tensor_tensor(y, u[:, k:k + TB], conv_w[:, k, c:c + 1], y, ALU.mult, ALU.add))
                    wait_unit(dve, b, U_CONV + 4 * c + 2)
                    step(v.tensor_tensor(y, y, banks[bk + 2], ALU.mult))
                    dve.wait_ge(s_conv_t, b * 4 + c + 1)
                    link(v.scalar_tensor_tensor(conv_g[q], conv_t[q], 1.0, banks[bk + 3], ALU.add, ALU.mult))
                    link(v.scalar_tensor_tensor(y, y, 0.5, conv_g[q], ALU.mult, ALU.mult))
                    split_y(c, y, s_ye)

                def pool_pre(g):
                    q, w = g % 2, 2 << g
                    u, bufs = pool_u[q], (pool_s[q], pool_d[q])
                    step(v.tensor_copy(u[:, 0:16], pool_hist[:, g, :]))
                    dve.wait_ge(s_pool_u, b * 4 + g + 1)
                    sync()
                    step(v.tensor_copy(pool_hist[:, g, :], u[:, TB:TB + 16]))
                    src, off = u, 1
                    for level in range(g + 1):
                        dst = bufs[level % 2]
                        lo = 2 * off - 1
                        link(v.tensor_tensor(dst[:, lo:PW], src[:, lo:PW], src[:, lo - off:PW - off], ALU.add))
                        src, off = dst, 2 * off
                    link(v.tensor_tensor(src[:, 16:32], src[:, 16:32], corr[:, g, :], ALU.mult))
                    v.scalar_tensor_tensor(pool_diff[g][:, 16:PW], src[:, 16:PW], 1.0 / w, u[:, 16:PW],
                                           ALU.mult, ALU.subtract).then_inc(s_pool_diff, 1)
                    dve.wait_ge(s_pool_t, b * 4 + g + 1)
                    v.scalar_tensor_tensor(pool_g[q][:, 0:TB], pool_t[q][:, 0:TB], 1.0, banks[2 * q + 1],
                                           ALU.add, ALU.mult).then_inc(s_pool_gate, 1)

                def pool_end(g):
                    q = g % 2
                    dve.wait_ge(s_pm, b * 4 + g + 1)
                    dve.wait_ge(s_pool_gate, b * 4 + g + 1)
                    y = pool_t[q][:, 0:TB]
                    link(v.scalar_tensor_tensor(y, banks[4 + g], pool_sc[:, g:g + 1], pool_g[q][:, 0:TB],
                                                ALU.mult, ALU.mult))
                    split_y(4 + g, y, s_ye)

                pool_pre(0)
                for g in range(1, GROUPS):
                    pool_pre(g)
                    pool_end(g - 1)
                pool_end(GROUPS - 1)
                def residual0(n, tt):
                    wait_tile(dve, b, OUT0 + n, tt)
                    if n == 0:
                        dve.wait_ge(s_store[tt], b * 16 + 1)
                    c = slice(n * 512, n * 512 + 512)
                    v.tensor_tensor(res[:, tt, c], banks[4 * n + tt], xin[:, tt, c], ALU.add).then_inc(s_res, 1)

                for tt in range(TT):
                    residual0(0, tt)
                residual0(1, 0)
                residual0(1, 1)
                tile1 = b * 8 + TT
                scale(tile1, 1, res, 0)
                scale(tile1 + 1, 1, res, 1)
                residual0(1, 2)
                split_h(tile1, 0)
                residual0(1, 3)
                scale(tile1 + 2, 1, res, 2)
                split_h(tile1 + 1, 1)
                scale(tile1 + 3, 1, res, 3)
                split_h(tile1 + 2, 2)
                split_h(tile1 + 3, 3)
                dve.wait_ge(s_gmm, b + 1)
                step(v.tensor_scalar(row_u[:, :], banks[2][0:MH, :], ib, None, ALU.add))
                dve.wait_ge(s_row_abs, b + 1)
                step(v.tensor_scalar(row_m[:, :], banks[2][64:64 + MH, :], fb, 0.0, ALU.add, ALU.min))
                dve.wait_ge(s_row_ln, b + 1)
                sync()
                link(v.tensor_tensor(row_m[:, :], row_m[:, :], row_t[:, :], ALU.subtract))
                step(v.tensor_tensor_scan(row_c[:, :], chunk_mask[:, :], row_m[:, :], 0.0, ALU.mult, ALU.add))
                link(v.memset(row_t[:, :], 0.0))
                step(v.tensor_tensor(row_u[:, :], row_u[:, :], row_c[:, :], ALU.subtract))
                step(v.tensor_copy(row_t[:, 0:1], carry_b[:, :]))
                step(v.tensor_tensor(m_prev[:, 0:1], carry_m[:, :], carry_b[:, :], ALU.add))
                link(v.tensor_copy(row_t[:, P:TB:P], row_c[:, P - 1:TB - 1:P]))
                link(v.tensor_tensor_scan(row_m[:, :], row_t[:, :], row_u[:, :], carry_m[:, :], ALU.add, ALU.max))
                step(v.tensor_tensor(m_prev[:, 1:TT], row_m[:, P - 1:TB - 1:P], row_c[:, P - 1:TB - 1:P], ALU.add))
                step(v.tensor_copy(carry_m[:, :], row_m[:, TB - 1:TB]))
                step(v.tensor_copy(carry_b[:, :], row_c[:, TB - 1:TB]))
                step(v.tensor_scalar(gate_rows[:, 3, :], row_m[:, :], -1.0, None, ALU.mult))
                link(v.scalar_tensor_tensor(gate_rows[:, 1, :], row_c[:, :], -1.0, row_m[:, :],
                                            ALU.mult, ALU.subtract))
                by_chunk = lambda r: r.rearrange("h (c t) -> h c t", c=TT)
                v.tensor_tensor(by_chunk(gate_rows[:, 2, :]), by_chunk(row_u[:, :]),
                                row_m[:, P - 1:TB:P].unsqueeze(2).broadcast_to([MH, TT, P]), ALU.subtract)
                v.tensor_tensor(by_chunk(gate_rows[:, 0, :]), by_chunk(gate_rows[:, 3, :]),
                                m_prev[:, :].unsqueeze(2).broadcast_to([MH, TT, P]), ALU.add).then_inc(s_rows_end, 1)

                def mem_pre(c):
                    q, a = c % 2, slice(c * P, (c + 1) * P)
                    dve.wait_ge(s_bc[q], b * 96 + 48 * (c // 2) + 48)
                    step(v.tensor_tensor(row_bc[q], row_bc[q], causal[:, :].unsqueeze(1).broadcast_to([P, MH, P]), ALU.add))
                    dve.wait_ge(s_ma, b * 4 + c + 1)
                    v.tensor_copy(cols[:, q, :], banks[5][:, 256:268]).then_inc(s_mem_masked, 1)
                    if c:
                        dve.wait_ge(s_mb, b * 4 + c)
                    for g in range(2):
                        r = slice(64 * g, 64 * g + 64)
                        step(v.tensor_tensor(q_inter[r, g:MH:2, :], q_mem[r, :, a], inter_bc[q][r], ALU.mult))
                    dve.wait_ge(s_mem_masked, b * 4 + c + 1)
                    step(v.tensor_tensor(k_wr, banks[5][:, 0:256].rearrange("p (h d) -> p h d", h=MH),
                                         cols[:, q, MH:2 * MH].unsqueeze(2).broadcast_to([P, MH, MD]), ALU.mult))
                    dve.wait_ge(s_mem_exp, b * 4 + c + 1)
                    v.tensor_tensor(decay_w, banks[4].rearrange("p (h t) -> p h t", h=MH), decay_w,
                                    ALU.mult).then_inc(s_mem_scored, 1)

                def mem_post(c):
                    q = c % 2
                    dve.wait_ge(s_mb, b * 4 + c + 1)
                    step(v.tensor_copy(den[:, 0, :].rearrange("p (b i) -> p b i", b=2), pair_c[:, :, ME:2 * ME + 2:ME + 1]))
                    for i in range(2):
                        last = v.scalar_tensor_tensor(state[:, i, :], state[:, i, :], inter_bc[q][:, i, P - 1:P],
                                                      banks[3][:, 129 * i:129 * i + 129], ALU.mult, ALU.add)
                    last.then_inc(s_mem_state, 1)
                    sync()
                    link(v.scalar_tensor_tensor(den[:, 1, :], den[:, 0, :], -1.0, den[:, 0, :], ALU.mult, ALU.max))
                    link(v.tensor_tensor(den[:, 1, :], den[:, 1, :], cols[:, q, 2 * MH:3 * MH], ALU.max))
                    link(v.reciprocal(den[:, 1, :], den[:, 1, :]))
                    if c >= 2:
                        dve.wait_ge(s_mtr, b * 4 + c - 1)
                    for i in range(2):
                        last = v.tensor_tensor(mem_tok[q][:, 2 * i:2 * i + 2, :],
                                               pair_c[:, i, 0:2 * ME + 2].rearrange("p (h e) -> p h e", h=2)[:, :, 0:ME],
                                               den[:, 1, 2 * i:2 * i + 2].unsqueeze(2).broadcast_to([P, 2, ME]), ALU.mult)
                    last.then_inc(s_mem_normed, 1)

                for c in range(TT):
                    mem_pre(c)
                    mem_post(c)

                def att_add(p):
                    sbk, g, q = p // 2, p % 2, p % 2
                    dve.wait_ge(s_aa, b * 8 + p + 1)
                    if p >= 2:
                        dve.wait_ge(s_ab, b * 8 + p - 1)
                    sc, src = scores[:, 4 * q:4 * q + 4, :], pair_b[:, :, :].rearrange("p b (j k) -> p (b j) k", j=2)
                    bi = bias[:, 4 * g:4 * g + 4, :]
                    if sbk == 0:
                        v.scalar_tensor_tensor(sc[:, :, 0:P], src[:, :, 0:P], first[:, :], bi[:, :, 0:P], ALU.add, ALU.add)
                        v.tensor_tensor(sc[:, :, P:2 * P], src[:, :, P:2 * P], bi[:, :, P:2 * P],
                                        ALU.add).then_inc(s_att_added, 1)
                    else:
                        v.tensor_tensor(sc, src, bi, ALU.add).then_inc(s_att_added, 1)
                    dve.wait_ge(s_att_added, b * 8 + p + 1)
                    link(v.tensor_reduce(sm[:, q, 0:4], sc, AX.X, ALU.max))
                    link(v.scalar_tensor_tensor(sm[:, q, 4:8], sm[:, q, 0:4], -1.0, neg_sink[:, 4 * g:4 * g + 4],
                                                ALU.mult, ALU.min))
                    v.tensor_tensor(sm[:, q, 16:20], sm[:, q, 4:8], neg_sink[:, 4 * g:4 * g + 4],
                                    ALU.subtract).then_inc(s_att_max, 1)

                def att_sum(p):
                    dve.wait_ge(s_att_exp, b * 8 + p + 1)
                    r = inv_sum[:, p % 4, :]
                    link(v.tensor_tensor(r, sm[:, p % 2, 8:12], sm[:, p % 2, 12:16], ALU.add))
                    step(v.reciprocal(r, r))

                def att_norm(p):
                    g = p % 2
                    dve.wait_ge(s_ac, b * 8 + p + 1)
                    if p >= 2 and g == 0:
                        dve.wait_ge(s_att_tr, b * 4 + p // 2)
                    by_head = lambda r: r[:, 256 * g:256 * g + 256].rearrange("p (j d) -> p j d", j=4)
                    v.tensor_tensor(by_head(att_tok), by_head(banks[2]),
                                    inv_sum[:, p % 4, :].unsqueeze(2).broadcast_to([P, 4, HD]),
                                    ALU.mult).then_inc(s_att_normed, 1)

                for s in range(12):
                    if 2 <= s < PIECES + 2:
                        p = s - 2
                        dve.wait_ge(s_ab, b * 8 + p + 1)
                        if p >= 2:
                            dve.wait_ge(s_ac, b * 8 + p - 1)
                        v.tensor_copy(probs_t[:, p % 2, 1, :], pair_c[:, 1, :]).then_inc(s_att_pv, 1)
                    if 3 <= s < PIECES + 3:
                        att_norm(s - 3)
                    if 1 <= s < PIECES + 1:
                        att_sum(s - 1)
                    if s < PIECES:
                        att_add(s)
                    if s < 8 and s % 2 == 1:
                        j = s // 2
                        if j == 0:
                            dve.wait_ge(s_mem_out, b * 4 + 4)
                        dve.wait_ge(s_gate_t, b * 12 + s + 1)
                        step(v.scalar_tensor_tensor(gate_a, gate_tanh[0], 1.0, mixed[:, 4 + j, :], ALU.add, ALU.mult))
                        v.scalar_tensor_tensor(gate_b, gate_tanh[1], 1.0, banks[1], ALU.add, ALU.mult).then_inc(s_gated, 1)
                        dve.wait_ge(s_gated, b * 8 + j + 1)
                        link(v.scalar_tensor_tensor(gate_a, gate_a, 0.25, gate_b, ALU.mult, ALU.mult))
                        split_y(4 + j, gate_a, s_yo)
                    if s >= 8:
                        dve.wait_ge(s_gate_t, b * 12 + s + 1)
                        v.scalar_tensor_tensor(att_gate[:, s - 8, :], gate_tanh[s % 2], 1.0, banks[s % 2],
                                               ALU.add, ALU.mult).then_inc(s_gated, 1)
                dve.wait_ge(s_gated, b * 8 + 8)
                dve.wait_ge(s_att_out, b * 4 + 4)
                for j in range(4):
                    g = att_gate[:, j, :]
                    link(v.scalar_tensor_tensor(g, mixed[:, j, :], 0.5, g, ALU.mult, ALU.mult))
                    split_y(j, g, s_yo)
                def residual1(n, tt):
                    wait_tile(dve, b, OUT2 + n, tt)
                    c = slice(n * 512, n * 512 + 512)
                    v.tensor_tensor(res[:, tt, c], banks[4 * n + tt], res[:, tt, c], ALU.add).then_inc(s_fin, 1)

                for tt in range(TT):
                    residual1(0, tt)
                norm(b * 8 + 2 * TT, 0, xin)
                for tt in range(TT):
                    residual1(1, tt)
                dve.wait_ge(s_sq, b * 24 + 8 + 24)
                rsqrt()
                for tt in range(TT):
                    v.scalar_tensor_tensor(res[:, tt, :], res[:, tt, :], root[:, 2, tt:tt + 1], gains[2][:, :],
                                           ALU.mult, ALU.mult).then_inc(s_norm, 1)
                step(v.memset(first[:, :], 0.0))
                step(v.memset(corr[:, :, :], 1.0))
                sync()
                assert count[0] == DVE_STEPS, count[0]


_INS = ['x', 'even_norm', 'even_w_in', 'even_conv_w', 'even_pool_w', 'even_pool_scale', 'even_w_out',
        'odd_norm', 'odd_w_in', 'odd_i_bias', 'odd_f_bias', 'odd_sinks', 'odd_w_out', 'final_norm']


def kernel(**inputs):
    import numpy as np
    import concourse.bacc as bacc
    from concourse.bass_utils import run_bass_kernel_spmd

    nc = bacc.Bacc("TRN2", target_bir_lowering=False, num_devices=1)
    arrays, args = {}, []
    for name in _INS:
        a = np.ascontiguousarray(inputs[name])
        arrays[f"in_{name}"] = a
        args.append(nc.dram_tensor(f"in_{name}", a.shape, mybir.dt.from_np(a.dtype), kind="ExternalInput").ap())
    args.append(nc.dram_tensor("result", (1, S, D), F32, kind="ExternalOutput").ap())
    trunk(nc, *args)
    r = run_bass_kernel_spmd(nc, [arrays], core_ids=[0])
    return r.results[0]["result"]
```
